# Optimizing a Trainium2 kernel written in Bass

```python
import jax, jax.numpy as jnp
from jax import lax
import numpy as np

D_MODEL = 1024
BATCH = 1
SEQ = 512
DEPTH = 1

CHUNK = 64
A_HEADS = 8
A_HEAD_DIM = 64
A_WIDTH = A_HEADS * A_HEAD_DIM
A_LEFT_CHUNKS = 8
A_BAND = (A_LEFT_CHUNKS + 1) * CHUNK
REL_CLIP = 128
B_BLOCK = 128
B_GROUPS = 4
B_WIDTH = D_MODEL // 2
B_GROUP_DIM = B_WIDTH // B_GROUPS
C_WIDTH = D_MODEL // 2
C_BLOCKS = 8
C_BLOCK_DIM = C_WIDTH // C_BLOCKS
CONV_WIDTH = 4
LRU_C = 8.0
N_BRANCH = 3
IN_COLS = 3 * A_WIDTH + 2 * B_WIDTH + 2 * C_WIDTH + N_BRANCH * D_MODEL
N_GROUPS = 4
EXPERTS_PER_GROUP = 4
N_EXPERTS = N_GROUPS * EXPERTS_PER_GROUP
TOP_K = 2
D_EXPERT = D_MODEL // 2
EPS = 1e-6

kernel_name = 'hybrid_streaming_gated_trunk'

def rms_norm(x, g):
    x32 = x.astype(jnp.float32)
    y = x32 * lax.rsqrt(jnp.mean(x32 * x32, axis=-1, keepdims=True) + EPS)
    return (y * g.astype(jnp.float32)).astype(x.dtype)

def chunked_rel_attention(q, k, v, rel_bias):
    b, s, _ = q.shape
    nc = s // CHUNK
    shp = (b, nc, CHUNK, A_HEADS, A_HEAD_DIM)
    q = q.reshape(shp)
    pad = ((0, 0), (A_LEFT_CHUNKS, 0), (0, 0), (0, 0), (0, 0))
    kp = jnp.pad(k.reshape(shp), pad)
    vp = jnp.pad(v.reshape(shp), pad)
    k_band = jnp.concatenate([kp[:, j:j + nc] for j in range(A_LEFT_CHUNKS + 1)], axis=2)
    v_band = jnp.concatenate([vp[:, j:j + nc] for j in range(A_LEFT_CHUNKS + 1)], axis=2)
    scores = jnp.einsum('bcqhd,bckhd->bhcqk', q, k_band).astype(jnp.float32) * (A_HEAD_DIM ** -0.5)
    q_pos = A_LEFT_CHUNKS * CHUNK + jnp.arange(CHUNK)
    k_pos = jnp.arange(A_BAND)
    rel = jnp.clip(q_pos[:, None] - k_pos[None, :], -REL_CLIP, REL_CLIP) + REL_CLIP
    bias = rel_bias.astype(jnp.float32)[:, rel]
    key_chunk = jnp.arange(nc)[:, None] - A_LEFT_CHUNKS + k_pos[None, :] // CHUNK
    valid = key_chunk >= 0
    scores = jnp.where(valid[None, None, :, None, :], scores + bias[None, :, None], -1e30)
    probs = jax.nn.softmax(scores, axis=-1).astype(v.dtype)
    out = jnp.einsum('bhcqk,bckhd->bcqhd', probs, v_band)
    return out.reshape(b, s, A_WIDTH)

def chunked_spatial_gating(u, v, norm_g, w_s, b_s):
    b, s, _ = u.shape
    nb = s // B_BLOCK
    u = jax.nn.gelu(u)
    v = rms_norm(jax.nn.gelu(v), norm_g).reshape(b, nb, B_BLOCK, B_GROUPS, B_GROUP_DIM)
    causal = jnp.tril(jnp.ones((B_BLOCK, B_BLOCK), dtype=bool))
    w = jnp.where(causal[None], w_s, jnp.zeros_like(w_s))
    mixed = jnp.einsum('gts,bnsgc->bntgc', w, v) + b_s.T[None, None, :, :, None]
    return u * mixed.reshape(b, s, B_WIDTH)

def causal_depthwise_conv(x, w, bias):
    s = x.shape[1]
    xp = jnp.pad(x, ((0, 0), (CONV_WIDTH - 1, 0), (0, 0)))
    return sum(xp[:, j:j + s] * w[j] for j in range(CONV_WIDTH)) + bias

def block_diag_linear(x, w, bias):
    b, s, _ = x.shape
    y = jnp.einsum('bshi,hij->bshj', x.reshape(b, s, C_BLOCKS, C_BLOCK_DIM), w)
    return y.reshape(b, s, C_WIDTH) + bias

def _lin_rec_combine(left, right):
    a1, b1 = left
    a2, b2 = right
    return a1 * a2, a2 * b1 + b2

def rg_lru(x, w_a, b_a, w_x, b_x, lam):
    r = jax.nn.sigmoid(block_diag_linear(x, w_a, b_a)).astype(jnp.float32)
    i = jax.nn.sigmoid(block_diag_linear(x, w_x, b_x))
    log_a = -LRU_C * r * jax.nn.softplus(-lam.astype(jnp.float32))
    a = jnp.exp(log_a)
    mult = jnp.sqrt(jnp.maximum(-jnp.expm1(2.0 * log_a), 0.0))
    bterm = mult * (i * x).astype(jnp.float32)
    _, h = lax.associative_scan(_lin_rec_combine, (a, bterm), axis=1)
    return h.astype(x.dtype)

def hybrid_mixer(xn, w_in, b_gate, rel_bias, sgu_norm_g, sgu_w, sgu_b, conv_w, conv_b,
                 rg_wa, rg_ba, rg_wx, rg_bx, rg_lambda, w_branch, w_out):
    b, s, _ = xn.shape
    proj = xn @ w_in
    cuts = [A_WIDTH, 2 * A_WIDTH, 3 * A_WIDTH,
            3 * A_WIDTH + B_WIDTH, 3 * A_WIDTH + 2 * B_WIDTH,
            3 * A_WIDTH + 2 * B_WIDTH + C_WIDTH, 3 * A_WIDTH + 2 * B_WIDTH + 2 * C_WIDTH]
    q, k, v, u, sv, xg, xr, gl = jnp.split(proj, cuts, axis=-1)
    a_out = chunked_rel_attention(q, k, v, rel_bias)
    b_out = chunked_spatial_gating(u, sv, sgu_norm_g, sgu_w, sgu_b)
    c_out = jax.nn.gelu(xg) * rg_lru(causal_depthwise_conv(xr, conv_w, conv_b),
                                     rg_wa, rg_ba, rg_wx, rg_bx, rg_lambda)
    gates = jax.nn.sigmoid(gl.reshape(b, s, N_BRANCH, D_MODEL) + b_gate)
    merged = (gates[:, :, 0] * (a_out @ w_branch[0])
              + gates[:, :, 1] * (b_out @ w_branch[1])
              + gates[:, :, 2] * (c_out @ w_branch[2]))
    return merged @ w_out

def hierarchical_moe(x, wg, bg, we, be, w_gate, w_up, w_down):
    b, s, d = x.shape
    xt = x.reshape(b * s, d)
    g_logits = (xt @ wg + bg).astype(jnp.float32)
    g_probs = jax.nn.softmax(g_logits, axis=-1)
    g_idx = jnp.argmax(g_logits, axis=-1)
    g_w = jnp.take_along_axis(g_probs, g_idx[:, None], axis=-1)
    e_logits = (xt @ we + be).astype(jnp.float32).reshape(-1, N_GROUPS, EXPERTS_PER_GROUP)
    e_logits = jnp.take_along_axis(e_logits, g_idx[:, None, None], axis=1)[:, 0]
    e_probs = jax.nn.softmax(e_logits, axis=-1)
    top_p, top_i = lax.top_k(e_probs, TOP_K)
    top_p = top_p / jnp.sum(top_p, axis=-1, keepdims=True)
    expert_id = g_idx[:, None] * EXPERTS_PER_GROUP + top_i
    combine = jnp.sum(jax.nn.one_hot(expert_id, N_EXPERTS, dtype=jnp.float32)
                      * (g_w * top_p)[..., None], axis=1).astype(x.dtype)
    y = jnp.zeros_like(xt)
    for e in range(N_EXPERTS):
        h = jax.nn.silu(xt @ w_gate[e]) * (xt @ w_up[e])
        y = y + combine[:, e:e + 1] * (h @ w_down[e])
    return y.reshape(b, s, d)

def setup_inputs(seed: int = 0) -> dict:
    key = jax.random.key(seed)
    ks = jax.random.split(key, 26)
    f32 = jnp.float32
    L = DEPTH

    def nrm(k, shape, scale):
        return jax.random.normal(k, shape, f32) * scale

    u_lam = jax.random.uniform(ks[14], (L, C_WIDTH), f32, 0.9, 0.999)
    a0 = u_lam ** (1.0 / LRU_C)
    rg_lambda = jnp.log(a0) - jnp.log1p(-a0)
    return {
        'x': nrm(ks[0], (BATCH, SEQ, D_MODEL), 1.0),
        'norm1_g': 1.0 + nrm(ks[1], (L, D_MODEL), 0.02),
        'w_in': nrm(ks[2], (L, D_MODEL, IN_COLS), D_MODEL ** -0.5),
        'b_gate': nrm(ks[3], (L, N_BRANCH, D_MODEL), 0.02),
        'rel_bias': nrm(ks[4], (L, A_HEADS, 2 * REL_CLIP + 1), 0.1),
        'sgu_norm_g': 1.0 + nrm(ks[5], (L, B_WIDTH), 0.02),
        'sgu_w': nrm(ks[6], (L, B_GROUPS, B_BLOCK, B_BLOCK), 0.5 * B_BLOCK ** -0.5),
        'sgu_b': 1.0 + nrm(ks[7], (L, B_GROUPS, B_BLOCK), 0.02),
        'conv_w': nrm(ks[8], (L, CONV_WIDTH, C_WIDTH), CONV_WIDTH ** -0.5),
        'conv_b': nrm(ks[9], (L, C_WIDTH), 0.02),
        'rg_wa': nrm(ks[10], (L, C_BLOCKS, C_BLOCK_DIM, C_BLOCK_DIM), C_BLOCK_DIM ** -0.5),
        'rg_ba': nrm(ks[11], (L, C_WIDTH), 0.02),
        'rg_wx': nrm(ks[12], (L, C_BLOCKS, C_BLOCK_DIM, C_BLOCK_DIM), C_BLOCK_DIM ** -0.5),
        'rg_bx': nrm(ks[13], (L, C_WIDTH), 0.02),
        'rg_lambda': rg_lambda,
        'w_branch': nrm(ks[15], (L, N_BRANCH, A_WIDTH, D_MODEL), A_WIDTH ** -0.5),
        'w_out': nrm(ks[16], (L, D_MODEL, D_MODEL), D_MODEL ** -0.5),
        'norm2_g': 1.0 + nrm(ks[17], (L, D_MODEL), 0.02),
        'router_grp_w': nrm(ks[18], (L, D_MODEL, N_GROUPS), D_MODEL ** -0.5),
        'router_grp_b': nrm(ks[19], (L, N_GROUPS), 0.01),
        'router_exp_w': nrm(ks[20], (L, D_MODEL, N_EXPERTS), D_MODEL ** -0.5),
        'router_exp_b': nrm(ks[21], (L, N_EXPERTS), 0.01),
        'exp_w_gate': nrm(ks[22], (L, N_EXPERTS, D_MODEL, D_EXPERT), D_MODEL ** -0.5),
        'exp_w_up': nrm(ks[23], (L, N_EXPERTS, D_MODEL, D_EXPERT), D_MODEL ** -0.5),
        'exp_w_down': nrm(ks[24], (L, N_EXPERTS, D_EXPERT, D_MODEL), D_EXPERT ** -0.5),
        'final_norm_g': 1.0 + nrm(ks[25], (D_MODEL,), 0.02),
    }

def reference(x, norm1_g, w_in, b_gate, rel_bias, sgu_norm_g, sgu_w, sgu_b, conv_w, conv_b,
              rg_wa, rg_ba, rg_wx, rg_bx, rg_lambda, w_branch, w_out, norm2_g,
              router_grp_w, router_grp_b, router_exp_w, router_exp_b,
              exp_w_gate, exp_w_up, exp_w_down, final_norm_g):
    for l in range(DEPTH):
        xn = rms_norm(x, norm1_g[l])
        x = x + hybrid_mixer(xn, w_in[l], b_gate[l], rel_bias[l], sgu_norm_g[l], sgu_w[l], sgu_b[l],
                             conv_w[l], conv_b[l], rg_wa[l], rg_ba[l], rg_wx[l], rg_bx[l],
                             rg_lambda[l], w_branch[l], w_out[l])
        xn = rms_norm(x, norm2_g[l])
        x = x + hierarchical_moe(xn, router_grp_w[l], router_grp_b[l], router_exp_w[l], router_exp_b[l],
                                 exp_w_gate[l], exp_w_up[l], exp_w_down[l])
    return rms_norm(x, final_norm_g)


_drawn_inputs = setup_inputs


def setup_inputs(seed=0):
    import zlib

    import numpy as np

    out = dict(_drawn_inputs(seed))
    spreads = {}
    factors = {'norm1_g': 2.689,
     'b_gate': 8.0,
     'rel_bias': 7.631,
     'sgu_norm_g': 51.718,
     'sgu_b': 20.055,
     'rg_ba': 48.481,
     'rg_bx': 41.308,
     'router_grp_b': 28.368,
     'router_exp_b': 44.904,
     'final_norm_g': 7.862,
     'conv_b': 4.464,
     'norm2_g': 8.0}
    for name, (base, spread) in spreads.items():
        noise = np.random.default_rng([zlib.crc32(name.encode()), seed]).standard_normal(out[name].shape)
        drawn = base * np.exp(spread * noise) if base else spread * noise
        out[name] = __import__('jax').numpy.asarray(drawn.astype(out[name].dtype))
    for name, factor in factors.items():
        out[name] = (out[name] * factor).astype(out[name].dtype)
    return out
```

```python
from contextlib import ExitStack

import concourse.bass as bass
from concourse import mybir

F32 = mybir.dt.float32
F32R = mybir.dt.float32r
BF16 = mybir.dt.bfloat16
I32 = mybir.dt.int32
ALU = mybir.AluOpType
ACT = mybir.ActivationFunctionType
AX = mybir.AxisListType

P = 128
TOK = 512
NT = TOK // P
D = 1024
KD = D // P
AW = 512
HEADS = 8
DH = AW // HEADS
CHUNK = 64
NPAIR = AW // P
CLIP = 128
LRU_C = 8.0
CONV = 4
NG = 4
EPG = 4
NE = NG * EPG
DE = D // 2
EPS = 1e-6
NEG = -1e30

Q0, K0, V0, U0, SV0, XG0, XR0, GL0 = (AW * i for i in range(8))

HI_SLOTS = 4
RAW_MIX = 4
RAW_EXP = 6
AHEAD = 3
PER_PAIR = 5
PER_OUT = 9
B_SV = 0
B_V = 4
B_PAIR = 8
B_GATE = B_PAIR + PER_PAIR * NPAIR
B_OUT = B_GATE + PER_OUT * NPAIR
B_EXP = B_OUT + 8
PER_TILE = 12
XR, KK, QQ, UU, XG = range(PER_PAIR)
BRANCH_ORDER = (2, 1, 0)

PAR_LAM, PAR_CB, PAR_BA, PAR_BX, PAR_CW, PAR_GATE = (NPAIR * n for n in (0, 1, 2, 3, 4, 8))
N_PAR = PAR_GATE + 3 * KD

OVER = 7
MAX_TILES = NE + OVER
SLOT_TILES = MAX_TILES + 1


def on_pool(r):
    return r % 3 == 1


LO_DVE_0 = 16


def pool_before(r):
    return sum(on_pool(x) for x in range(r))


def build(nc, a, out):
    slots = nc.dram_tensor("slots", [SLOT_TILES * P, D], F32, kind="Internal").ap()
    toep = nc.dram_tensor("toep", [HEADS, P, 3 * P], F32, kind="Internal").ap()

    w_in = a["w_in"][0]
    w_branch = a["w_branch"][0]
    w_out = a["w_out"][0]
    w_g, w_u, w_d = a["exp_w_gate"][0], a["exp_w_up"][0], a["exp_w_down"][0]

    ctx = ExitStack()
    with ctx:
        def sem(name):
            return ctx.enter_context(nc.semaphore(name))

        def psum(name, shape, dt=F32):
            return ctx.enter_context(nc.psum_tensor(name, shape, dt))

        def sb(stack, name, shape, dt=F32):
            return stack.enter_context(nc.sbuf_tensor(name, shape, dt))

        raw = sb(ctx, "raw", [P, RAW_EXP, 1024])
        w_hi = sb(ctx, "w_hi", [P, HI_SLOTS, 1024], F32R)
        w_lo = sb(ctx, "w_lo", [P, HI_SLOTS, 1024], F32R)
        ident = sb(ctx, "ident", [P, P])
        tile_table = sb(ctx, "tile_table", [P, 32], I32)
        stat = sb(ctx, "stat", [P, 8, NT])
        minus_half = sb(ctx, "minus_half", [P, 1])
        w_first = sb(ctx, "w_first", [P, 2, NT])
        slot_idx = sb(ctx, "slot_idx", [P, 2 * NT], I32)
        par = sb(ctx, "par", [P, N_PAR])
        chan = sb(ctx, "chan", [P, 8, NPAIR])
        att = sb(ctx, "att", [P, 2, 4])
        macc_odd = sb(ctx, "macc_odd", [P, TOK])
        macc_term = sb(ctx, "macc_term", [P, TOK])

        AREA_A, AREA_B = 30 * 256, 34 * 256

        with ExitStack() as s0:
            sb(s0, "pad_a0", [P, AREA_A + AREA_B])
            x0 = sb(s0, "x0", [P, NT, D])
            x0_sq = sb(s0, "x0_sq", [P, D])
            g1_rows = sb(s0, "g1_rows", [P, D])

        with ExitStack() as s1:
            v_rows = sb(s1, "v_rows", [P, NT, AW])
            bias = sb(s1, "bias", [P, HEADS, 2 * P])
            qT = sb(s1, "qT", [P, 2, TOK])
            kT = sb(s1, "kT", [P, 2, TOK])
            probs = sb(s1, "probs", [P, 2, TOK])
            probsT = sb(s1, "probsT", [P, TOK])
            sv_rows = sb(s1, "sv_rows", [P, NT, AW])
            sgu_wT = sb(s1, "sgu_wT", [P, 4, P])
            sgu_b_sb = sb(s1, "sgu_b_sb", [P, 4, P])
            sgu_g_sb = sb(s1, "sgu_g_sb", [P, AW])
            wa_diag = sb(s1, "wa_diag", [P, NPAIR, P])
            wx_diag = sb(s1, "wx_diag", [P, NPAIR, P])
            xrT = sb(s1, "xrT", [P, CONV - 1 + TOK])
            conv = sb(s1, "conv", [P, TOK])
            rgate = sb(s1, "rgate", [P, TOK])
            igate = sb(s1, "igate", [P, TOK])
            decay = sb(s1, "decay", [P, TOK])
            gx = sb(s1, "gx", [P, TOK])
            gu = sb(s1, "gu", [P, TOK])
            sb(s1, "pad_b1", [P, AREA_B - (NT * AW + 4 * P + 4 * P + AW + 2 * NPAIR * P + CONV - 1 + 7 * TOK)])
            br_hi = sb(s1, "br_hi", [P, 3, NPAIR, TOK], F32R)
            br_lo = sb(s1, "br_lo", [P, 3, NPAIR, TOK], F32R)
            xn_hi = sb(s1, "xn_hi", [P, KD, TOK], F32R)
            xn_lo = sb(s1, "xn_lo", [P, KD, TOK], F32R)

        with ExitStack() as s2:
            x_rows = sb(s2, "x_rows", [P, NT, D])
            sb(s2, "pad_a2", [P, AREA_A - NT * D])
            mg_hi = sb(s2, "mg_hi", [P, KD, TOK], F32R)
            mg_lo = sb(s2, "mg_lo", [P, KD, TOK], F32R)
            sb(s2, "pad_b2", [P, AREA_B - 2 * KD * TOK])
            xn2 = sb(s2, "xn2", [P, NT, D])
            g2_rows = sb(s2, "g2_rows", [P, D])
            gf_rows = sb(s2, "gf_rows", [P, D])
            xn2T = sb(s2, "xn2T", [P, 2, D])
            route = sb(s2, "route", [P, 26, NT * NE])
            tri = sb(s2, "tri", [P, 2, P], BF16)
            picked_bf = sb(s2, "picked_bf", [P, NT, NE], BF16)
            router_w = sb(s2, "router_w", [P, KD, NG + NE])
            router_b = sb(s2, "router_b", [P, NG + NE])
            xT_hi = sb(s2, "xT_hi", [P, KD, P], F32R)
            xT_lo = sb(s2, "xT_lo", [P, KD, P], F32R)
            hT_hi = sb(s2, "hT_hi", [P, DE // P, P], F32R)
            hT_lo = sb(s2, "hT_lo", [P, DE // P, P], F32R)
            silu = sb(s2, "silu", [P, DE])
            hid = sb(s2, "hid", [P, DE])
            x_tile = sb(s2, "x_tile", [P, D])
            y_tile = sb(s2, "y_tile", [P, D])
        with ExitStack() as s3:
            sb(s3, "pad_a3", [P, AREA_A + AREA_B])
            sb(s3, "pad_x3", [P, NT * D])
            sb(s3, "pad_g3", [P, 2 * D])
            y_got = sb(s3, "y_got", [P, 4, D])
        with ExitStack() as s4:
            sb(s4, "pad_a4", [P, NT * D])
            y_more = sb(s4, "y_more", [P, 4, D])

        gate_buf = raw[:, 4:6, :].rearrange("p a (b n) -> p (a b) n", n=TOK)

        def turned_x(t):
            return ps[:, 2 * t:2 * t + 2, :].rearrange("p a (b n) -> p (a b) n", n=P)

        def macc_of(k):
            return gate_buf[:, 3, :] if k % 2 == 0 else macc_odd[:, :]

        def y_lo(t):
            return y_got[:, t, :]

        def y_hi(t):
            return y_more[:, t, :]

        ps = psum("ps", [P, 8, 512])

        S = {n: sem(n) for n in (
            "x0_sq_done x0_stat x0_rstd x0_norm x0_turned xn_hi_done xn_done "
            "hi_act lo_pool lo_dve w_used taken "
            "ident_done consts_pool consts_dve zero_done zeros_stored "
            "g1_in chan_in diag_in sgu_in relb_in toep_rev toep_out bias_in bias_done route_in g2_in "
            "sgu_raw sguT_ps sguT_done mask_done sv_sq sv_stat sv_rstd sv_done sp_exp sp_done conv_done gates_ps gates_done "
            "decay_done mult_in mult_done aux_taken c_mid b_mid ch bh c_ready b_ready mix_ps "
            "scores_ps biased exped inv_done normed probsT_ps probsT_done out_ps a_hi a_ready "
            "gate_ready wb_taken macc_done mg_hi_done mg_done x_again x2_done x2_sq x2_stat x2_rstd xn2_done "
            "xn2T_ps xn2T_done logits_ps gexp_in gexp_done eexp_done picked counts_ps routed scattered tab "
            "x_in xT_ps xT_hi_done xT_done silu_done hid_done hT_ps hT_hi_done hT_done y_act y_dve y_stored all_stored "
            "y_got_in y_sum y_sq y_stat y_rstd y_norm y_out dve_chain").split()}
        raw_in = [sem(f"raw_in{s}") for s in range(RAW_EXP)]
        x0_in = [sem(f"x0_in{s}") for s in range(NT)]
        got_in = [sem(f"got_in{s}") for s in range(NT)]

        def raw_slot(b):
            return b % RAW_MIX if b < B_EXP else (b - B_EXP) % RAW_EXP

        def raw_count(b):
            s = raw_slot(b)
            if b < B_EXP:
                return 16 * (b // RAW_MIX + 1)
            before = B_EXP // RAW_MIX if s < RAW_MIX else 0
            return 16 * (before + (b - B_EXP) // RAW_EXP + 1)

        def loop_block(i, r):
            return i * PER_TILE + (B_EXP + 8 + r - PER_TILE)

        def loop_raw_slot(r):
            return (8 + r) % RAW_EXP

        def loop_raw_count(i, r):
            before = B_EXP // RAW_MIX if loop_raw_slot(r) < RAW_MIX else 0
            per_tile = PER_TILE // RAW_EXP
            return i * (16 * per_tile) + 16 * (before + (8 + r) // RAW_EXP + 1 - per_tile)

        POOL_TILE = pool_before(PER_TILE)
        DVE_TILE = PER_TILE - POOL_TILE

        def lo_wait(eng, b):
            if b < B_EXP:
                eng.wait_ge(S["lo_pool"], b + 1)
            elif on_pool(b - B_EXP):
                eng.wait_ge(S["lo_pool"], B_EXP + pool_before(b - B_EXP + 1))
            else:
                eng.wait_ge(S["lo_dve"], LO_DVE_0 + b - B_EXP + 1 - pool_before(b - B_EXP + 1))

        def lo_wait_loop(eng, i, r):
            tile = -1 if r < 0 else 0
            c = 8 + r % PER_TILE
            if on_pool(c):
                eng.wait_ge(S["lo_pool"], i * POOL_TILE + (B_EXP + pool_before(c + 1) + (tile - 1) * POOL_TILE))
            else:
                eng.wait_ge(S["lo_dve"],
                            i * DVE_TILE + (LO_DVE_0 + c + 1 - pool_before(c + 1) + (tile - 1) * DVE_TILE))

        def split_hi(b):
            nc.scalar.wait_ge(raw_in[raw_slot(b)], raw_count(b))
            if b >= HI_SLOTS:
                nc.scalar.wait_ge(S["w_used"], b - HI_SLOTS + 1)
            nc.scalar.activation(w_hi[:, b % HI_SLOTS, :], raw[:, raw_slot(b), :], ACT.Copy)\
                .then_inc(S["hi_act"], 1)

        def split_hi_loop(i, r):
            nc.scalar.wait_ge(raw_in[loop_raw_slot(r)], loop_raw_count(i, r))
            nc.scalar.wait_ge(S["w_used"], loop_block(i, r) - (HI_SLOTS - 1))
            nc.scalar.activation(w_hi[:, (8 + r) % HI_SLOTS, :], raw[:, loop_raw_slot(r), :],
                                 ACT.Copy).then_inc(S["hi_act"], 1)

        def split_lo(eng, b):
            eng.wait_ge(S["hi_act"], b + 1)
            eng.tensor_tensor(w_lo[:, b % HI_SLOTS, :], raw[:, raw_slot(b), :],
                              w_hi[:, b % HI_SLOTS, :].bitcast(F32), ALU.subtract)\
               .then_inc(S["lo_pool"] if b < B_EXP or on_pool(b - B_EXP) else S["lo_dve"], 1)

        def split_lo_loop(eng, i, r):
            eng.wait_ge(S["hi_act"], loop_block(i, r) + 1)
            eng.tensor_tensor(w_lo[:, (8 + r) % HI_SLOTS, :], raw[:, loop_raw_slot(r), :],
                              w_hi[:, (8 + r) % HI_SLOTS, :].bitcast(F32), ALU.subtract)\
               .then_inc(S["lo_pool"] if on_pool(8 + r) else S["lo_dve"], 1)

        def pair_block(j, r):
            return B_PAIR + PER_PAIR * j + r

        def out_block(m, r):
            return B_GATE + PER_OUT * m + r

        block = ctx.enter_context(nc.Block())

        @block.sync
        def _(sp):
            def rows2(w, k0, c0):
                return w[k0 * P:(k0 + 2) * P, c0:c0 + 512].rearrange("(k p) n -> p k n", p=P)

            def load(b, src, n_k):
                if b < B_EXP:
                    if b >= RAW_MIX:
                        lo_wait(sp, b - RAW_MIX)
                elif b < B_EXP + RAW_MIX:
                    lo_wait(sp, b - RAW_MIX)
                elif b < B_EXP + RAW_EXP:
                    sp.wait_ge(S["mg_done"], KD)
                else:
                    lo_wait(sp, b - RAW_EXP)
                dst = raw[:, raw_slot(b), :].rearrange("p (k n) -> p k n", k=n_k)
                sp.dma_start(dst, src).then_inc(raw_in[raw_slot(b)], 16)

            for t in range(NT):
                sp.dma_start(x0[:, t, :], a["x"][0, t * P:(t + 1) * P, :]).then_inc(x0_in[t], 16)
            for kp in range(4):
                load(B_SV + kp, rows2(w_in, 2 * kp, SV0), 2)
            for kp in range(4):
                load(B_V + kp, rows2(w_in, 2 * kp, V0), 2)

            def cols(c0):
                return w_in[:, c0:c0 + P].rearrange("(k p) n -> p k n", p=P)

            sp.wait_ge(S["zero_done"], 1)
            for j in range(NPAIR):
                for r, c0 in enumerate((XR0, K0, Q0, U0, XG0)):
                    load(pair_block(j, r), cols(c0 + j * P), KD)
                for n in range(j * SLOT_TILES // NPAIR, (j + 1) * SLOT_TILES // NPAIR):
                    sp.dma_start(slots[n * P:(n + 1) * P, :], raw[:, 4, :]).then_inc(S["zeros_stored"], 16)
            for m in range(NPAIR):
                if m == 2:
                    sp.wait_ge(S["a_ready"], NPAIR)
                    sp.dma_start(x_rows[:, :, :], a["x"][0].rearrange("(t p) n -> p t n", p=P))\
                      .then_inc(S["x_again"], 16)
                for o, br in enumerate(BRANCH_ORDER):
                    for c in range(2):
                        load(out_block(m, 3 * o + c), cols(GL0 + br * D + (2 * m + c) * P), KD)
                    load(out_block(m, 3 * o + 2),
                         w_branch[br, :, 2 * m * P:2 * (m + 1) * P].rearrange("(k p) n -> p k n", p=P), 4)
            for n in range(2):
                for kp in range(4):
                    load(B_OUT + 4 * n + kp, rows2(w_out, 2 * kp, 512 * n), 2)
            for r in range(4):
                load(B_EXP + r, rows2(w_g[0], 2 * r, 0), 2)
            for r in range(4, 8):
                load(B_EXP + r, rows2(w_u[0], 2 * (r - 4), 0), 2)

            sp.wait_ge(S["scattered"], 16 * 2 * NT)
            sp.dma_start(x_tile[:, :], slots[0:P, :]).then_inc(S["x_in"], 16)
            sp.wait_ge(S["xT_ps"], 1)
            sp.dma_start(x_tile[:, :], slots[P:2 * P, :]).then_inc(S["x_in"], 16)
            sp.wait_ge(S["tab"], 1)
            tiles = sp.value_load(tile_table[0:1, 0:1], min_val=NE, max_val=MAX_TILES)

            def load_loop(i, r, src):
                lo_wait_loop(sp, i, r - RAW_EXP)
                sp.dma_start(raw[:, loop_raw_slot(r), :].rearrange("p (k n) -> p k n", k=2), src)\
                  .then_inc(raw_in[loop_raw_slot(r)], 16)

            with sp.Fori(1, tiles) as i:
                e = sp.value_load(tile_table[0:1, bass.ds(i + 1, 1)], min_val=0, max_val=NE - 1)
                before = sp.value_load(tile_table[0:1, bass.ds(i, 1)], min_val=0, max_val=NE - 1)
                for kp in range(4):
                    load_loop(i, kp, rows2(w_g[e], 2 * kp, 0))
                sp.wait_ge(S["xT_ps"], i + 1)
                sp.dma_start(x_tile[:, :], slots[bass.ds((i + 1) * P, P), :]).then_inc(S["x_in"], 16)
                for kp in range(4):
                    load_loop(i, 4 + kp, rows2(w_u[e], 2 * kp, 0))
                for n in range(2):
                    for kp in range(2):
                        load_loop(i, 8 + 2 * n + kp, rows2(w_d[before], 2 * kp, 512 * n))
            last = sp.value_load(tile_table[0:1, bass.ds(tiles, 1)], min_val=0, max_val=NE - 1)
            for n in range(2):
                for kp in range(2):
                    load_loop(tiles, 2 * n + kp, rows2(w_d[last], 2 * kp, 512 * n))

            for t in range(NT):
                sp.wait_ge(S["y_norm"], t + 1)
                sp.dma_start(out[0, t * P:(t + 1) * P, :], y_lo(t)).then_inc(S["y_out"], 16)
            sp.wait_ge(S["y_out"], 16 * NT)

        @block.gpsimd
        def _(pool):
            pool.memset(ident[:, :], 0.0).then_inc(S["ident_done"], 1)
            pool.memset(minus_half[:, :], -0.5).then_inc(S["consts_pool"], 1)
            pool.wait_ge(S["ident_done"], 1)
            pool.affine_select(out=ident[:, :], in_=ident[:, :], compare_op=ALU.not_equal, fill=1.0, base=0,
                               pattern=[[-1, P]], channel_multiplier=1).then_inc(S["ident_done"], 1)
            pool.wait_ge(S["consts_pool"], 1)
            for t in range(NT):
                pool.wait_ge(S["x0_stat"], t + 1)
                pool.tensor_tensor(stat[:, 1, t:t + 1], stat[:, 0, t:t + 1], minus_half[:, :], ALU.pow)\
                    .then_inc(S["x0_rstd"], 1)
            for b in range(AHEAD):
                split_lo(pool, b)
            pool.wait_ge(S["toep_rev"], 2)
            pool.dma_start(toep, probs[0:HEADS, 0, 0:3 * P].unsqueeze(1).to_broadcast([HEADS, P, 3 * P])).then_inc(S["toep_out"], 16)
            pool.wait_ge(S["toep_out"], 16)
            pool.dma_start(bias[:, :, :], bass.AP(toep.tensor, P - 1, [[3 * P - 1, P], [3 * P * P, HEADS], [1, 2 * P]]))\
                .then_inc(S["bias_in"], 16)
            pool.memset(gate_buf[:, 0:2, :], 0.0).then_inc(S["zero_done"], 1)
            for b in range(AHEAD, B_PAIR + AHEAD):
                split_lo(pool, b)
                if b == AHEAD + 1:
                    pool.wait_ge(S["bias_in"], 16)
                    pool.memset(bias[0:CHUNK, :, 3 * CHUNK:4 * CHUNK], NEG).then_inc(S["bias_done"], 1)
                    pool.wait_ge(S["sguT_done"], 1)
                    pool.affine_select(out=sgu_wT[:, :, :], in_=sgu_wT[:, :, :], compare_op=ALU.is_ge, fill=0.0,
                                       base=0, pattern=[[0, 4], [1, P]], channel_multiplier=-1)\
                        .then_inc(S["mask_done"], 1)
            for t in range(NT):
                pool.wait_ge(S["sv_stat"], t + 1)
                pool.tensor_tensor(stat[:, 3, t:t + 1], stat[:, 2, t:t + 1], minus_half[:, :], ALU.pow)\
                    .then_inc(S["sv_rstd"], 1)

            def normalise(jp, u):
                n = 8 * jp + u
                w = P * (u % NT + 1)
                pool.wait_ge(S["inv_done"], n + 1)
                pool.tensor_scalar(probs[:, n % 2, 0:w], probs[:, n % 2, 0:w], att[:, n % 2, 2:3], None,
                                   ALU.mult).then_inc(S["normed"], 1)

            for j in range(NPAIR):
                for r in range(PER_PAIR):
                    split_lo(pool, pair_block(j, r) + AHEAD)
                    for n in range(3 * r, 3 * r + 3):
                        if j > 0 and n < 8:
                            normalise(j - 1, n)
            for m in range(NPAIR):
                n = 0
                for r in range(PER_OUT):
                    b = out_block(m, r)
                    split_lo(pool, b + AHEAD)
                    if m == 0:
                        for _ in range(2 if r % 3 == 2 else 3):
                            if n < 8:
                                normalise(NPAIR - 1, n)
                            n += 1
            for b in range(B_OUT, B_EXP - AHEAD):
                split_lo(pool, b + AHEAD)
            pool.memset(tri[:, :, :], 1.0).then_inc(S["consts_pool"], 1)
            pool.wait_ge(S["consts_pool"], 2)
            pool.affine_select(out=tri[:, 0, :], in_=tri[:, 0, :], compare_op=ALU.is_gt, fill=0.0, base=0,
                               pattern=[[1, P]], channel_multiplier=-1).then_inc(S["consts_pool"], 1)
            for r, (base, pattern) in enumerate((
                    (NG, [[0, NT], [-1, NG]]), (NE, [[0, NT], [-1, NE]]),
                    (0, [[P, NE]]), (0, [[1, 8]]), (0, [[1, NE]]))):
                n = 1
                for _, c in pattern:
                    n *= c
                pool.iota(route[:, 20 + r, 0:n], pattern=pattern, base=base, channel_multiplier=0,
                          allow_small_or_imprecise_dtypes=True)\
                    .then_inc(S["consts_pool"], 1)
            for t in range(NT):
                pool.wait_ge(S["x2_stat"], t + 1)
                pool.tensor_tensor(stat[:, 5, t:t + 1], stat[:, 4, t:t + 1], minus_half[:, :], ALU.pow)\
                    .then_inc(S["x2_rstd"], 1)
            split_lo(pool, B_EXP + 1)
            pool.wait_ge(S["zeros_stored"], 16 * SLOT_TILES)
            pool.wait_ge(S["xn2_done"], NT)
            pool.wait_ge(S["routed"], 1)
            for t in range(NT):
                for k in range(2):
                    pool.indirect_dma_start(
                        slots, bass.IndirectOffsetOnAxis(ap=slot_idx[:, 2 * t + k:2 * t + k + 1], axis=0),
                        xn2[:, t, :], None).then_inc(S["scattered"], 16)
            for r in range(AHEAD, 8 + AHEAD):
                if r < 8:
                    if on_pool(r):
                        split_lo(pool, B_EXP + r)
            pool.wait_ge(S["tab"], 1)
            tiles = pool.value_load(tile_table[0:1, 0:1], min_val=NE, max_val=MAX_TILES)
            for r in range(8, 8 + AHEAD):
                if on_pool(r):
                    split_lo_loop(pool, 1, r - 8)
            with pool.Fori(1, tiles) as i:
                for r in range(PER_TILE):
                    if on_pool(8 + r + AHEAD):
                        split_lo_loop(pool, i, r + AHEAD)
            if on_pool(8 + AHEAD):
                split_lo_loop(pool, tiles, AHEAD)
            pool.wait_ge(S["all_stored"], 1)
            for t in range(NT):
                for k, dst in enumerate((y_lo(t), y_hi(t))):
                    pool.indirect_dma_start(
                        dst, None, slots,
                        bass.IndirectOffsetOnAxis(ap=slot_idx[:, 2 * t + k:2 * t + k + 1], axis=0))\
                        .then_inc(got_in[t], 16)
            for t in range(NT):
                pool.wait_ge(S["y_stat"], t + 1)
                pool.tensor_tensor(stat[:, 7, t:t + 1], stat[:, 6, t:t + 1], minus_half[:, :], ALU.pow)\
                    .then_inc(S["y_rstd"], 1)

        @block.scalar
        def _(act):
            act.dma_start(g1_rows[:, :], a["norm1_g"][0:1, :].broadcast_to([P, D])).then_inc(S["g1_in"], 16)
            act.dma_start(probs[0:HEADS, 1, 0:2 * CLIP + 1], a["rel_bias"][0]).then_inc(S["relb_in"], 16)
            act.dma_start(sgu_g_sb[:, :], a["sgu_norm_g"][0:1, :].broadcast_to([P, AW])).then_inc(S["sgu_in"], 16)
            act.dma_start(sgu_b_sb[:, :, :].rearrange("p g t -> p (g t)"),
                          a["sgu_b"].rearrange("a g t -> a (g t)").broadcast_to([P, 4 * P]))\
               .then_inc(S["sgu_in"], 16)
            act.dma_start(gu[:, :].rearrange("t (g s) -> t g s", g=4), a["sgu_w"][0].rearrange("g t s -> t g s"))\
               .then_inc(S["sgu_raw"], 16)
            for r, src in ((PAR_LAM, a["rg_lambda"]), (PAR_CB, a["conv_b"]), (PAR_BA, a["rg_ba"]),
                           (PAR_BX, a["rg_bx"]), (PAR_CW, a["conv_w"][0]), (PAR_GATE, a["b_gate"][0])):
                n = src.shape[0] * src.shape[1] // P
                act.dma_start(gx[r:r + n, 0:P], src.rearrange("a (c p) -> (a c) p", p=P)).then_inc(S["chan_in"], 16)
            act.wait_ge(S["consts_dve"], 2)
            for w, dst in (("rg_wa", wa_diag), ("rg_wx", wx_diag)):
                for h in range(2):
                    act.dma_start(dst[h * 64:(h + 1) * 64, :, h * 64:(h + 1) * 64],
                                  a[w][0].rearrange("(c h) i j -> h i c j", h=2)[h]).then_inc(S["diag_in"], 16)

            for t in range(NT):
                act.wait_ge(x0_in[t], 16)
                if t > 0:
                    act.wait_ge(S["x0_sq_done"], t)
                act.activation(x0_sq[:, :], x0[:, t, :], ACT.Square, accum_out=stat[:, 0, t:t + 1])\
                   .then_inc(S["x0_sq_done"], 1)
            for b in range(AHEAD):
                split_hi(b)
            for t in range(NT):
                act.wait_ge(S["x0_turned"], t + 1)
                act.activation(xn_hi[:, :, t * P:(t + 1) * P], turned_x(t), ACT.Copy)\
                   .then_inc(S["xn_hi_done"], 1)
            act.wait_ge(S["sp_exp"], 1)
            act.activation(chan[:, 1, :], chan[:, 0, :], ACT.Exp, scale=-1.0).then_inc(S["sp_exp"], 1)

            for b in range(B_SV, B_V):
                split_hi(b + AHEAD)
            for b in range(B_V, B_PAIR):
                split_hi(b + AHEAD)
                t = b - B_V
                if t == 0:
                    act.wait_ge(S["w_used"], B_V)
                act.activation(sv_rows[:, t, :], ps[:, t, :], ACT.Gelu_apprx_tanh).then_inc(S["taken"], 1)
            for t in range(NT):
                act.wait_ge(S["taken"], t + 1)
                if t > 0:
                    act.wait_ge(S["sv_sq"], t)
                else:
                    act.wait_ge(S["sguT_done"], 1)
                act.activation(gx[:, :], sv_rows[:, t, :], ACT.Square, accum_out=stat[:, 2, t:t + 1])\
                   .then_inc(S["sv_sq"], 1)
            act.wait_ge(S["w_used"], B_PAIR)
            for t in range(NT):
                act.activation(v_rows[:, t, :], ps[:, 4 + t, :], ACT.Copy).then_inc(S["taken"], 1)

            def exps(n):
                w = P * (n % NT + 1)
                act.wait_ge(S["biased"], n + 1)
                act.activation(probs[:, n % 2, 0:w], probs[:, n % 2, 0:w], ACT.Exp, bias=att[:, n % 2, 0:1],
                               accum_out=att[:, n % 2, 1:2]).then_inc(S["exped"], 1)

            def take_probsT(n):
                w = P * (n % NT + 1)
                act.wait_ge(S["probsT_ps"], n + 1)
                if n >= 1:
                    act.wait_ge(S["out_ps"], n)
                act.activation(probsT[:, 0:w], ps[:, 6, 0:w], ACT.Copy).then_inc(S["probsT_done"], 1)

            def attention(jp, u):
                if 3 <= u < 11:
                    take_probsT(8 * jp + u - 3)
                if u < 8:
                    exps(8 * jp + u)

            def a_out_hi(jp):
                act.wait_ge(S["out_ps"], 8 * (jp + 1))
                act.activation(br_hi[:, 0, jp, :], ps[:, 7, :], ACT.Copy).then_inc(S["a_hi"], 1)

            def take(b, dst, func):
                act.wait_ge(S["w_used"], b + 1)
                act.activation(dst, ps[:, b % 2, :], func).then_inc(S["taken"], 1)

            def c_hi(j):
                act.wait_ge(S["c_mid"], j + 1)
                act.activation(br_hi[:, 2, j, :], gx[:, :], ACT.Copy).then_inc(S["ch"], 1)

            def b_hi(j):
                act.wait_ge(S["b_mid"], j + 1)
                act.activation(br_hi[:, 1, j, :], gu[:, :], ACT.Copy).then_inc(S["bh"], 1)

            for j in range(NPAIR):
                for r in range(PER_PAIR):
                    b = pair_block(j, r)
                    split_hi(b + AHEAD)
                    if r == XR and j > 0:
                        if j > 1:
                            act.wait_ge(S["c_ready"], j - 1)
                        take(b - 1, gx[:, :], ACT.Gelu_apprx_tanh)
                    if r == KK:
                        if j > 0:
                            act.wait_ge(S["conv_done"], j)
                        take(b - 1, xrT[:, CONV - 1:], ACT.Copy)
                    if r == QQ:
                        take(b - 1, kT[:, j % 2, :], ACT.Copy)
                    if r == UU:
                        take(b - 1, qT[:, j % 2, :], ACT.Copy)
                    for n in range(3 * r, 3 * r + 3):
                        if j > 0:
                            attention(j - 1, n)
                    if r == QQ and j > 0:
                        c_hi(j - 1)
                        b_hi(j - 1)
                    if r == UU:
                        if j > 0:
                            a_out_hi(j - 1)
                        act.wait_ge(S["gates_ps"], 2 * j + 2)
                        if j > 0:
                            act.wait_ge(S["b_mid"], j)
                        act.activation(rgate[:, :], ps[:, 2, :], ACT.Sigmoid, bias=par[:, PAR_BA + j:PAR_BA + j + 1])\
                           .then_inc(S["gates_done"], 1)
                        act.activation(igate[:, :], ps[:, 3, :], ACT.Sigmoid, bias=par[:, PAR_BX + j:PAR_BX + j + 1])\
                           .then_inc(S["gates_done"], 1)
                        act.wait_ge(S["gates_done"], 2 * j + 1)
                        act.wait_ge(S["sp_done"], 1)
                        act.activation(decay[:, :], rgate[:, :], ACT.Exp, scale=chan[:, 3, j:j + 1])\
                           .then_inc(S["decay_done"], 1)
                        act.wait_ge(S["decay_done"], 2 * j + 1)
                        act.activation(rgate[:, :], rgate[:, :], ACT.Tanh, scale=chan[:, 2, j:j + 1])\
                           .then_inc(S["decay_done"], 1)
                    if r == XG:
                        if j > 0:
                            act.wait_ge(S["b_ready"], j)
                        else:
                            act.wait_ge(S["sguT_ps"], 1)
                        act.wait_ge(S["mult_in"], j + 1)
                        act.activation(rgate[:, :], rgate[:, :], ACT.Sqrt).then_inc(S["mult_done"], 1)
                        take(b - 1, gu[:, :], ACT.Gelu_apprx_tanh)

            def gate(m, o, c):
                g = 6 * m + 2 * o + c
                br = BRANCH_ORDER[o]
                act.wait_ge(S["w_used"], out_block(m, 3 * o + c) + 1)
                if g >= 3:
                    act.wait_ge(S["wb_taken"], g - 2)
                else:
                    act.wait_ge(S["zeros_stored"], 16 * SLOT_TILES)
                act.activation(gate_buf[:, g % 3, :], ps[:, c, :], ACT.Sigmoid,
                               bias=par[:, PAR_GATE + KD * br + 2 * m + c:PAR_GATE + KD * br + 2 * m + c + 1]).then_inc(S["gate_ready"], 1)

            def mg_hi_part(k):
                act.wait_ge(S["macc_done"], k + 1)
                act.activation(mg_hi[:, k, :], macc_of(k), ACT.Copy).then_inc(S["mg_hi_done"], 1)

            for m in range(NPAIR):
                n = 0
                for r in range(PER_OUT):
                    b = out_block(m, r)
                    split_hi(b + AHEAD)
                    if m == 0 and r == 0:
                        act.wait_ge(S["c_ready"], NPAIR - 1)
                        take(b - 1, gx[:, :], ACT.Gelu_apprx_tanh)
                    if r > 0 and (r - 1) % 3 < 2:
                        gate(m, (r - 1) // 3, (r - 1) % 3)
                    if m == 0:
                        for _ in range(2 if r % 3 == 2 else 3):
                            if n < 11:
                                attention(NPAIR - 1, n)
                            n += 1
                        if r == 1:
                            c_hi(NPAIR - 1)
                            b_hi(NPAIR - 1)
                        if r == 5:
                            a_out_hi(NPAIR - 1)
                    if r == 0 and m > 0:
                        for c in range(2):
                            mg_hi_part(2 * (m - 1) + c)
            for b in range(B_OUT, B_EXP):
                split_hi(b + AHEAD)
                if b == B_OUT:
                    for c in range(2):
                        mg_hi_part(KD - 2 + c)
                    act.dma_start(g2_rows[:, :], a["norm2_g"][0:1, :].broadcast_to([P, D])).then_inc(S["g2_in"], 16)
                    act.dma_start(router_w[:, :, 0:NG], a["router_grp_w"][0].rearrange("(k p) n -> p k n", p=P))\
                       .then_inc(S["route_in"], 16)
                    act.dma_start(router_w[:, :, NG:], a["router_exp_w"][0].rearrange("(k p) n -> p k n", p=P))\
                       .then_inc(S["route_in"], 16)
                    act.dma_start(router_b[:, 0:NG], a["router_grp_b"][0:1, :].broadcast_to([P, NG]))\
                       .then_inc(S["route_in"], 16)
                    act.dma_start(router_b[:, NG:], a["router_exp_b"][0:1, :].broadcast_to([P, NE]))\
                       .then_inc(S["route_in"], 16)
                    act.dma_start(gf_rows[:, :],
                                  a["final_norm_g"].rearrange("(a n) -> a n", a=1).broadcast_to([P, D]))\
                       .then_inc(S["route_in"], 16)
            for t in range(NT):
                act.wait_ge(S["x2_done"], NT + t + 1)
                if t > 0:
                    act.wait_ge(S["x2_sq"], t)
                act.activation(y_tile[:, :], x_rows[:, t, :], ACT.Square, accum_out=stat[:, 4, t:t + 1])\
                   .then_inc(S["x2_sq"], 1)
            for t in range(NT):
                act.wait_ge(S["xn2T_ps"], t + 1)
                if t >= 2:
                    act.wait_ge(S["logits_ps"], t - 1)
                act.activation(xn2T[:, t % 2, :], ps[:, 4 + 2 * (t % 2):6 + 2 * (t % 2), :].rearrange(
                    "p a n -> p (a n)"), ACT.Copy).then_inc(S["xn2T_done"], 1)
            act.wait_ge(S["gexp_in"], 1)
            act.activation(route[:, 4, 0:4 * NG], route[:, 3, 0:4 * NG], ACT.Exp).then_inc(S["gexp_done"], 1)
            act.wait_ge(S["gexp_in"], 2)
            act.activation(route[:, 12, :], route[:, 11, :], ACT.Exp).then_inc(S["eexp_done"], 1)

            def xT_hi_part(n):
                act.wait_ge(S["xT_ps"], n)
                act.activation(xT_hi[:, :, :].rearrange("p k n -> p (k n)"),
                               ps[:, 3:5, :].rearrange("p a n -> p (a n)"), ACT.Copy)\
                   .then_inc(S["xT_hi_done"], 1)

            def silu_part(used):
                act.wait_ge(S["w_used"], used)
                act.activation(silu[:, :], ps[:, 0, :], ACT.Silu).then_inc(S["silu_done"], 1)

            def hT_hi_part(n):
                act.wait_ge(S["hT_ps"], n)
                act.activation(hT_hi[:, :, :].rearrange("p k n -> p (k n)"), ps[:, 2, :], ACT.Copy)\
                   .then_inc(S["hT_hi_done"], 1)

            def y_part(used, n):
                act.wait_ge(S["w_used"], used)
                act.wait_ge(S["y_stored"], n * 16)
                act.activation(y_tile[:, 0:512], ps[:, 5, :], ACT.Copy).then_inc(S["y_act"], 1)
                act.wait_ge(S["y_act"], n + 1)
                act.wait_ge(S["y_dve"], n + 1)
                act.dma_start(slots[bass.ds((n - 1) * P, P), :], y_tile[:, :]).then_inc(S["y_stored"], 16)

            act.sem_inc(S["y_stored"], 16)
            act.sem_inc(S["y_act"], 1)
            xT_hi_part(1)
            for r in range(8):
                if r + AHEAD < 8:
                    split_hi(B_EXP + r + AHEAD)
                elif r + AHEAD == 8:
                    split_hi_loop(1, 0)
                else:
                    split_hi_loop(1, r + AHEAD - 8)
                if r == 4:
                    silu_part(B_EXP + 4)
            act.wait_ge(S["tab"], 1)
            tiles = act.value_load(tile_table[0:1, 0:1], min_val=NE, max_val=MAX_TILES)
            xT_hi_part(2)
            with act.Fori(1, tiles) as i:
                for r in range(PER_TILE):
                    split_hi_loop(i, r + AHEAD)
                    if r == 4:
                        act.wait_ge(S["hid_done"], i)
                        silu_part(loop_block(i, 4))
                    if r == 5:
                        hT_hi_part(i)
                    if r == 9:
                        xT_hi_part(i + 2)
                y_part(loop_block(i, PER_TILE), i)
            hT_hi_part(tiles)
            split_hi_loop(tiles, AHEAD)
            y_part(loop_block(tiles, 4), tiles)
            act.wait_ge(S["y_stored"], tiles * 16 + 16)
            act.sem_inc(S["all_stored"], 1)
            for t in range(NT):
                act.wait_ge(S["y_sum"], 2 * t + 2)
                if t > 0:
                    act.wait_ge(S["y_sq"], t)
                act.activation(xn2[:, 0, :], y_lo(t), ACT.Square, accum_out=stat[:, 6, t:t + 1])\
                   .then_inc(S["y_sq"], 1)

        @block.tensor
        def _(pe):
            def three(dst, hi_l, lo_l, hi_r, lo_r, start, stop):
                pe.matmul(dst, hi_l, hi_r, start=start, stop=False)
                pe.matmul(dst, hi_l, lo_r, start=False, stop=False)
                return pe.matmul(dst, lo_l, hi_r, start=False, stop=stop)

            def w(b, part):
                return (w_hi, w_lo)[part][:, b % HI_SLOTS, :]

            pe.wait_ge(S["ident_done"], 2)
            for t in range(NT):
                pe.wait_ge(S["x0_norm"], t + 1)
                for k in range(KD):
                    mm = pe.transpose(ps[:, 2 * t + k // 4, (k % 4) * P:(k % 4 + 1) * P], x0[:, t, k * P:(k + 1) * P], ident[:, :])
                mm.then_inc(S["x0_turned"], 1)
            pe.wait_ge(S["xn_done"], NT)
            pe.wait_ge(S["chan_in"], 96)
            pe.transpose(ps[:, 6, 0:N_PAR], gx[0:N_PAR, 0:P], ident[0:N_PAR, 0:N_PAR])
            pe.wait_ge(S["sgu_raw"], 16)
            for g in range(4):
                mm = pe.transpose(ps[:, 7, g * P:(g + 1) * P], gu[:, g * P:(g + 1) * P], ident[:, :])
            mm.then_inc(S["sguT_ps"], 1)

            def rows_block(b, kp, lhs_hi, lhs_lo, bank):
                lo_wait(pe, b)
                for t in range(NT):
                    for kk in range(2):
                        k = 2 * kp + kk
                        mm = three(ps[:, bank + t, :], lhs_hi[:, k, t * P:(t + 1) * P],
                                   lhs_lo[:, k, t * P:(t + 1) * P],
                                   w(b, 0)[:, kk * 512:(kk + 1) * 512], w(b, 1)[:, kk * 512:(kk + 1) * 512],
                                   k == 0, k == KD - 1)
                mm.then_inc(S["w_used"], 1)

            for kp in range(4):
                rows_block(B_SV + kp, kp, xn_hi, xn_lo, 0)
            pe.wait_ge(S["sguT_done"], 1)
            for kp in range(4):
                rows_block(B_V + kp, kp, xn_hi, xn_lo, 4)

            def cols_piece(b, bank, ks):
                for k in ks:
                    mm = three(ps[:, bank, :], w(b, 0)[:, k * P:(k + 1) * P], w(b, 1)[:, k * P:(k + 1) * P],
                               xn_hi[:, k, :], xn_lo[:, k, :], k == 0, k == KD - 1)
                if ks[-1] == KD - 1:
                    mm.then_inc(S["w_used"], 1)

            PIECES = ((0, 1, 2), (3, 4, 5), (6, 7))

            def scores(n):
                jp, u = n // 8, n % 8
                h, i = u // NT, u % NT
                hp = slice(DH * h, DH * (h + 1))
                if n == 0:
                    pe.wait_ge(S["taken"], 8)
                if u == 0:
                    pe.wait_ge(S["taken"], pair_block(jp, QQ) + 1)
                if n >= 2:
                    pe.wait_ge(S["biased"], n - 1)
                pe.matmul(ps[:, 4 + n % 2, 0:(i + 1) * P], qT[hp, jp % 2, i * P:(i + 1) * P],
                          kT[hp, jp % 2, 0:(i + 1) * P], start=True, stop=True).then_inc(S["scores_ps"], 1)

            def turn_probs(n):
                i = n % NT
                pe.wait_ge(S["normed"], n + 1)
                if n >= 1:
                    pe.wait_ge(S["probsT_done"], n)
                for kt in range(i + 1):
                    mm = pe.transpose(ps[:, 6, kt * P:(kt + 1) * P], probs[:, n % 2, kt * P:(kt + 1) * P],
                                      ident[:, :])
                mm.then_inc(S["probsT_ps"], 1)

            def times_v(n):
                jp, u = n // 8, n % 8
                h, i = u // NT, u % NT
                pe.wait_ge(S["probsT_done"], n + 1)
                if u == 0 and jp > 0:
                    pe.wait_ge(S["a_ready"], jp)
                for kt in range(i + 1):
                    mm = pe.matmul(ps[DH * h:DH * (h + 1), 7, i * P:(i + 1) * P],
                                   v_rows[:, kt, (2 * jp + h) * DH:(2 * jp + h + 1) * DH],
                                   probsT[:, kt * P:(kt + 1) * P], start=(kt == 0), stop=(kt == i))
                mm.then_inc(S["out_ps"], 1)

            def attention(jp, u):
                if u < 8:
                    scores(8 * jp + u)
                if 3 <= u < 11:
                    times_v(8 * jp + u - 3)
                if 2 <= u < 10:
                    turn_probs(8 * jp + u - 2)

            for j in range(NPAIR):
                for r in range(PER_PAIR):
                    b = pair_block(j, r)
                    lo_wait(pe, b)
                    pe.wait_ge(S["taken"], b - 1 if b >= B_PAIR + 2 else 4)
                    for piece, ks in enumerate(PIECES):
                        cols_piece(b, b % 2, ks)
                        if j > 0:
                            attention(j - 1, 3 * r + piece)
                        if r == QQ and piece == 1:
                            pe.wait_ge(S["conv_done"], j + 1)
                            pe.wait_ge(S["diag_in"], 64)
                            if j > 0:
                                pe.wait_ge(S["b_mid"], j)
                            pe.matmul(ps[:, 2, :], wa_diag[:, j, :], conv[:, :], start=True, stop=True)\
                              .then_inc(S["gates_ps"], 1)
                            pe.matmul(ps[:, 3, :], wx_diag[:, j, :], conv[:, :], start=True, stop=True)\
                              .then_inc(S["gates_ps"], 1)
                        if r == XG and piece == 0:
                            pe.wait_ge(S["gates_done"], 2 * j + 2)
                            pe.wait_ge(S["sv_done"], NT)
                            pe.wait_ge(S["mask_done"], 1)
                            for n in range(NT):
                                mm = pe.matmul(ps[:, 2, n * P:(n + 1) * P], sv_rows[:, n, j * P:(j + 1) * P],
                                               sgu_wT[:, j, :], start=True, stop=True)
                            mm.then_inc(S["mix_ps"], 1)

            for m in range(NPAIR):
                n = 0
                for r in range(PER_OUT):
                    b = out_block(m, r)
                    o, c = r // 3, r % 3
                    br = BRANCH_ORDER[o]
                    lo_wait(pe, b)
                    if c < 2:
                        g = 6 * m + 2 * o + c
                        if g < 2:
                            pe.wait_ge(S["taken"], B_GATE - 1 + c)
                        else:
                            pe.wait_ge(S["gate_ready"], g - 1)
                        for ks in PIECES:
                            cols_piece(b, c, ks)
                            if m == 0 and n < 11:
                                attention(NPAIR - 1, n)
                            n += 1
                    else:
                        pe.wait_ge(S[("a_ready", "b_ready", "c_ready")[br]], NPAIR)
                        for c in range(2):
                            g = 6 * m + 2 * o + c
                            if g >= 2:
                                pe.wait_ge(S["wb_taken"], g - 1)
                            else:
                                pe.wait_ge(S["b_mid"], NPAIR)
                            for k in range(NPAIR):
                                at = k * 2 * P + c * P
                                mm = three(ps[:, 2 + c, :], w(b, 0)[:, at:at + P], w(b, 1)[:, at:at + P],
                                           br_hi[:, br, k, :], br_lo[:, br, k, :], k == 0, k == NPAIR - 1)
                            if c == 1:
                                mm.then_inc(S["w_used"], 1)
                            if m == 0 and n < 11:
                                attention(NPAIR - 1, n)
                            n += 1
            for n in range(2):
                for kp in range(4):
                    if n == 0:
                        pe.wait_ge(S["mg_done"], 2 * kp + 2)
                    rows_block(B_OUT + 4 * n + kp, kp, mg_hi, mg_lo, 4 - 4 * n)

            def logits(t):
                if t == 0:
                    pe.wait_ge(S["route_in"], 80)
                pe.wait_ge(S["xn2T_done"], t + 1)
                for k in range(KD):
                    mm = pe.matmul(ps[:, 0, t * 32:t * 32 + NG + NE], xn2T[:, t % 2, k * P:(k + 1) * P],
                                   router_w[:, k, :], start=(k == 0), stop=(k == KD - 1))
                mm.then_inc(S["logits_ps"], 1)

            for t in range(NT):
                pe.wait_ge(S["xn2_done"], t + 1)
                if t >= 2:
                    pe.wait_ge(S["xn2T_done"], t - 1)
                for k in range(KD):
                    mm = pe.transpose(ps[:, 4 + 2 * (t % 2) + k // 4, (k % 4) * P:(k % 4 + 1) * P],
                                      xn2[:, t, k * P:(k + 1) * P], ident[:, :])
                mm.then_inc(S["xn2T_ps"], 1)
                if t >= 1:
                    logits(t - 1)
            logits(NT - 1)
            pe.wait_ge(S["picked"], 1)
            pe.wait_ge(S["consts_pool"], 3)
            for t in range(NT):
                for s in range(t + 1):
                    pe.matmul(ps[:, 1, t * NE:(t + 1) * NE], tri[:, 0 if s == t else 1, :], picked_bf[:, s, :],
                              start=(s == 0), stop=(s == t))
            for s in range(NT):
                mm = pe.matmul(ps[:, 1, NT * NE:(NT + 1) * NE], tri[:, 1, :], picked_bf[:, s, :],
                               start=(s == 0), stop=(s == NT - 1))
            mm.then_inc(S["counts_ps"], 1)

            def turn_x(n):
                pe.wait_ge(S["x_in"], n * 16)
                for k in range(KD):
                    mm = pe.transpose(ps[:, 3 + k // 4, (k % 4) * P:(k % 4 + 1) * P],
                                      x_tile[:, k * P:(k + 1) * P], ident[:, :])
                mm.then_inc(S["xT_ps"], 1)

            def turn_h(n):
                pe.wait_ge(S["hid_done"], n)
                for k in range(DE // P):
                    mm = pe.transpose(ps[:, 2, k * P:(k + 1) * P], hid[:, k * P:(k + 1) * P], ident[:, :])
                mm.then_inc(S["hT_ps"], 1)

            def expert_block(slot, bank, k0, n_k, hi, lo):
                for kk in range(2):
                    k = k0 + kk
                    mm = three(ps[:, bank, :], hi[:, k, :], lo[:, k, :],
                               w_hi[:, slot, kk * 512:(kk + 1) * 512], w_lo[:, slot, kk * 512:(kk + 1) * 512],
                               k == 0, k == n_k - 1)
                mm.then_inc(S["w_used"], 1)

            turn_x(1)
            pe.wait_ge(S["xT_done"], 1)
            for r in range(8):
                lo_wait(pe, B_EXP + r)
                expert_block(r % HI_SLOTS, r // 4, 2 * (r % 4), KD, xT_hi, xT_lo)
            turn_x(2)
            pe.wait_ge(S["tab"], 1)
            tiles = pe.value_load(tile_table[0:1, 0:1], min_val=NE, max_val=MAX_TILES)
            with pe.Fori(1, tiles) as i:
                for r in range(PER_TILE):
                    if r == 0:
                        pe.wait_ge(S["xT_done"], i + 1)
                        pe.wait_ge(S["silu_done"], i)
                    if r == 4:
                        turn_h(i)
                    if r == 8:
                        turn_x(i + 2)
                        pe.wait_ge(S["hT_done"], i)
                    lo_wait_loop(pe, i, r)
                    slot = (8 + r) % HI_SLOTS
                    if r < 8:
                        expert_block(slot, r // 4, 2 * (r % 4), KD, xT_hi, xT_lo)
                    else:
                        expert_block(slot, 5 + (r - 8) // 2, 2 * (r % 2), DE // P, hT_hi, hT_lo)
            turn_h(tiles)
            pe.wait_ge(S["hT_done"], tiles)
            pe.wait_ge(S["y_act"], tiles)
            pe.wait_ge(S["y_dve"], tiles)
            for r in range(4):
                lo_wait_loop(pe, tiles, r)
                expert_block((8 + r) % HI_SLOTS, 5 + r // 2, 2 * (r % 2), DE // P, hT_hi, hT_lo)

        @block.vector
        def _(dve):
            chained = [0]

            def link(ins):
                chained[0] += 1
                ins.then_inc(S["dve_chain"], 1)
                dve.wait_ge(S["dve_chain"], chained[0])

            dve.sem_inc(S["lo_dve"], LO_DVE_0)
            dve.sem_inc(S["y_dve"], 1)
            dve.memset(wa_diag[:, :, :], 0.0).then_inc(S["consts_dve"], 1)
            dve.memset(wx_diag[:, :, :], 0.0).then_inc(S["consts_dve"], 1)
            dve.wait_ge(S["relb_in"], 16)
            dve.tensor_copy(probs[0:HEADS, 0, 0:P - 1],
                            probs[0:HEADS, 1, 2 * CLIP:2 * CLIP + 1].to_broadcast([HEADS, P - 1]))\
               .then_inc(S["toep_rev"], 1)
            dve.tensor_copy(probs[0:HEADS, 0, P - 1:3 * P], probs[0:HEADS, 1, 2 * CLIP::-1])\
               .then_inc(S["toep_rev"], 1)
            dve.wait_ge(S["g1_in"], 16)
            for t in range(NT):
                dve.wait_ge(S["x0_sq_done"], t + 1)
                dve.tensor_scalar(stat[:, 0, t:t + 1], stat[:, 0, t:t + 1], 1.0 / D, EPS, ALU.mult, ALU.add)\
                   .then_inc(S["x0_stat"], 1)
                dve.wait_ge(S["x0_rstd"], t + 1)
                dve.scalar_tensor_tensor(out=x0[:, t, :], in0=x0[:, t, :], scalar=stat[:, 1, t:t + 1],
                                         in1=g1_rows[:, :], op0=ALU.mult, op1=ALU.mult)\
                   .then_inc(S["x0_norm"], 1)
            for t in range(NT):
                dve.wait_ge(S["xn_hi_done"], t + 1)
                dve.tensor_tensor(xn_lo[:, :, t * P:(t + 1) * P], turned_x(t),
                                  xn_hi[:, :, t * P:(t + 1) * P].bitcast(F32), ALU.subtract)\
                   .then_inc(S["xn_done"], 1)
            dve.wait_ge(S["sguT_ps"], 1)
            link(dve.tensor_copy(par[:, :], ps[:, 6, 0:N_PAR]))
            dve.tensor_copy(sgu_wT[:, :, :].rearrange("p g t -> p (g t)"), ps[:, 7, :])\
               .then_inc(S["sguT_done"], 1)

            lam = par[:, PAR_LAM:PAR_LAM + NPAIR]
            mag, e1, s1, s2, acc = (chan[:, n, :] for n in (0, 1, 4, 5, 6))
            link(dve.tensor_scalar(mag, lam, -1.0, None, ALU.mult))
            dve.tensor_tensor(mag, lam, mag, ALU.max).then_inc(S["sp_exp"], 1)
            dve.wait_ge(S["sp_exp"], 2)
            link(dve.tensor_scalar(s2, e1, 2.0, None, ALU.add))
            link(dve.reciprocal(s1, s2))
            link(dve.tensor_tensor(s1, s1, e1, ALU.mult))
            link(dve.tensor_tensor(s2, s1, s1, ALU.mult))
            terms = 9
            link(dve.tensor_scalar(acc, s2, 1.0 / (2 * terms + 1), 1.0 / (2 * terms - 1), ALU.mult, ALU.add))
            for n in range(terms - 2, -1, -1):
                link(dve.tensor_tensor(acc, acc, s2, ALU.mult))
                link(dve.tensor_scalar(acc, acc, 1.0 / (2 * n + 1), None, ALU.add))
            link(dve.tensor_tensor(acc, acc, s1, ALU.mult))
            link(dve.tensor_scalar(mag, lam, -1.0, 0.0, ALU.mult, ALU.max))
            link(dve.scalar_tensor_tensor(out=acc, in0=acc, scalar=2.0, in1=mag, op0=ALU.mult, op1=ALU.add))
            dve.tensor_scalar(chan[:, 2, :], acc, LRU_C, None, ALU.mult).then_inc(S["sp_done"], 1)
            link(dve.tensor_scalar(chan[:, 3, :], acc, -LRU_C, None, ALU.mult))
            link(dve.memset(xrT[:, 0:CONV - 1], 0.0))

            dve.wait_ge(S["sgu_in"], 32)
            for t in range(NT):
                dve.wait_ge(S["sv_sq"], t + 1)
                dve.tensor_scalar(stat[:, 2, t:t + 1], stat[:, 2, t:t + 1], 1.0 / AW, EPS, ALU.mult, ALU.add)\
                   .then_inc(S["sv_stat"], 1)
            for t in range(NT):
                dve.wait_ge(S["sv_rstd"], t + 1)
                dve.scalar_tensor_tensor(out=sv_rows[:, t, :], in0=sv_rows[:, t, :],
                                         scalar=stat[:, 3, t:t + 1], in1=sgu_g_sb[:, :],
                                         op0=ALU.mult, op1=ALU.mult).then_inc(S["sv_done"], 1)

            def bias_and_max(n):
                h, i = n // NT, n % NT
                w, buf = P * (i + 1), n % 2
                dve.wait_ge(S["scores_ps"], n + 1)
                if n == 0:
                    dve.wait_ge(S["bias_done"], 1)
                if n >= 2:
                    dve.wait_ge(S["probsT_ps"], n - 1)
                near = min(2, i + 1) * P
                if w > near:
                    link(dve.tensor_scalar(probs[:, buf, 0:w - near], ps[:, 4 + buf, 0:w - near], DH ** -0.5,
                                           bias[:, h, 0:1], ALU.mult, ALU.add))
                link(dve.scalar_tensor_tensor(out=probs[:, buf, w - near:w], in0=ps[:, 4 + buf, w - near:w],
                                              scalar=DH ** -0.5, in1=bias[:, h, 2 * P - near:],
                                              op0=ALU.mult, op1=ALU.add))
                dve.tensor_reduce(att[:, buf, 0:1], probs[:, buf, 0:w], AX.X, ALU.max, negate=True)\
                   .then_inc(S["biased"], 1)

            def inverse(n):
                dve.wait_ge(S["exped"], n + 1)
                dve.reciprocal(att[:, n % 2, 2:3], att[:, n % 2, 1:2]).then_inc(S["inv_done"], 1)

            def attention(jp, u):
                if u < 8:
                    bias_and_max(8 * jp + u)
                    inverse(8 * jp + u)

            def a_out_lo(jp):
                dve.wait_ge(S["a_hi"], jp + 1)
                dve.tensor_tensor(br_lo[:, 0, jp, :], ps[:, 7, :], br_hi[:, 0, jp, :].bitcast(F32),
                                  ALU.subtract).then_inc(S["a_ready"], 1)

            def convolve(j):
                dve.wait_ge(S["taken"], pair_block(j, XR) + 1)
                if j > 0:
                    dve.wait_ge(S["c_mid"], j)
                link(dve.tensor_scalar(conv[:, :], xrT[:, 0:TOK], par[:, PAR_CW + j:PAR_CW + j + 1], None, ALU.mult))
                for k in range(1, CONV):
                    link(dve.scalar_tensor_tensor(out=conv[:, :], in0=xrT[:, k:k + TOK],
                                                  scalar=par[:, PAR_CW + NPAIR * k + j:PAR_CW + NPAIR * k + j + 1], in1=conv[:, :],
                                                  op0=ALU.mult, op1=ALU.add))
                dve.tensor_scalar(conv[:, :], conv[:, :], par[:, PAR_CB + j:PAR_CB + j + 1], None, ALU.add)\
                   .then_inc(S["conv_done"], 1)

            def recurrence_in(j):
                dve.wait_ge(S["gates_done"], 2 * j + 2)
                link(dve.tensor_tensor(igate[:, :], igate[:, :], conv[:, :], ALU.mult))
                dve.wait_ge(S["decay_done"], 2 * j + 2)
                link(dve.tensor_tensor(conv[:, :], decay[:, :], decay[:, :], ALU.mult))
                link(dve.scalar_tensor_tensor(out=rgate[:, :], in0=conv[:, :], scalar=1.0, in1=rgate[:, :],
                                              op0=ALU.add, op1=ALU.mult))
                dve.tensor_scalar(rgate[:, :], rgate[:, :], 0.0, None, ALU.max).then_inc(S["mult_in"], 1)

            def recurrence(j):
                dve.wait_ge(S["mult_done"], j + 1)
                link(dve.tensor_tensor(igate[:, :], igate[:, :], rgate[:, :], ALU.mult))
                link(dve.tensor_tensor_scan(out=conv[:, :], data0=decay[:, :], data1=igate[:, :], initial=0.0,
                                            op0=ALU.mult, op1=ALU.add))

            def c_out(j):
                dve.wait_ge(S["taken"], pair_block(j, XG) + 1)
                dve.tensor_tensor(gx[:, :], gx[:, :], conv[:, :], ALU.mult).then_inc(S["c_mid"], 1)

            def b_out(j):
                dve.wait_ge(S["mix_ps"], j + 1)
                dve.wait_ge(S["taken"], pair_block(j, UU) + 1)
                link(dve.tensor_tensor(rgate[:, :].rearrange("p (n t) -> p n t", n=NT),
                                       ps[:, 2, :].rearrange("p (n t) -> p n t", n=NT),
                                       sgu_b_sb[:, j, :].unsqueeze(1).to_broadcast([P, NT, P]), ALU.add))
                dve.tensor_tensor(gu[:, :], gu[:, :], rgate[:, :], ALU.mult).then_inc(S["b_mid"], 1)

            def lo_parts(j):
                dve.wait_ge(S["ch"], j + 1)
                dve.tensor_tensor(br_lo[:, 2, j, :], gx[:, :], br_hi[:, 2, j, :].bitcast(F32), ALU.subtract)\
                   .then_inc(S["c_ready"], 1)
                dve.wait_ge(S["bh"], j + 1)
                dve.tensor_tensor(br_lo[:, 1, j, :], gu[:, :], br_hi[:, 1, j, :].bitcast(F32), ALU.subtract)\
                   .then_inc(S["b_ready"], 1)

            for j in range(NPAIR):
                for r in range(PER_PAIR):
                    if r == XR and j > 0:
                        c_out(j - 1)
                    for n in range(3 * r, 3 * r + 3):
                        if n == 4:
                            convolve(j)
                        if j > 0:
                            attention(j - 1, n)
                    if r == UU:
                        if j > 0:
                            lo_parts(j - 1)
                            a_out_lo(j - 1)
                        recurrence_in(j)
                    if r == XG:
                        recurrence(j)
                        b_out(j)

            def gated(m, o, c):
                g = 6 * m + 2 * o + c
                k = 2 * m + c
                dve.wait_ge(S["w_used"], out_block(m, 3 * o + 2) + 1)
                dve.wait_ge(S["gate_ready"], g + 1)
                if o == 0:
                    if m > 0:
                        dve.wait_ge(S["mg_done"], k - 1)
                    dve.tensor_tensor(macc_of(k), ps[:, 2 + c, :], gate_buf[:, g % 3, :], ALU.mult)\
                       .then_inc(S["wb_taken"], 1)
                    return
                dve.tensor_tensor(macc_term[:, :], ps[:, 2 + c, :], gate_buf[:, g % 3, :], ALU.mult)\
                   .then_inc(S["wb_taken"], 1)
                dve.wait_ge(S["wb_taken"], g + 1)
                add = dve.tensor_tensor(macc_of(k), macc_of(k), macc_term[:, :], ALU.add)
                if o == 2:
                    add.then_inc(S["macc_done"], 1)
                    dve.wait_ge(S["macc_done"], k + 1)
                else:
                    link(add)

            def mg_lo_part(k):
                dve.wait_ge(S["mg_hi_done"], k + 1)
                dve.tensor_tensor(mg_lo[:, k, :], macc_of(k), mg_hi[:, k, :].bitcast(F32), ALU.subtract)\
                   .then_inc(S["mg_done"], 1)

            for m in range(NPAIR):
                n = 0
                for r in range(PER_OUT):
                    if m == 0 and r == 0:
                        c_out(NPAIR - 1)
                    if r % 3 == 0 and r > 0:
                        for c in range(2):
                            gated(m, r // 3 - 1, c)
                    if m == 0:
                        for _ in range(2 if r % 3 == 2 else 3):
                            if n < 8:
                                attention(NPAIR - 1, n)
                            n += 1
                        if r == 1:
                            lo_parts(NPAIR - 1)
                        if r == 5:
                            a_out_lo(NPAIR - 1)
                for c in range(2):
                    gated(m, 2, c)
                for c in range(2):
                    mg_lo_part(2 * m + c)
            dve.wait_ge(S["x_again"], 16)
            for n in range(2):
                dve.wait_ge(S["w_used"], B_OUT + 4 * (n + 1))
                for t in range(NT):
                    dve.tensor_tensor(x_rows[:, t, 512 * n:512 * (n + 1)], ps[:, (4 - 4 * n) + t, :],
                                      x_rows[:, t, 512 * n:512 * (n + 1)], ALU.add).then_inc(S["x2_done"], 1)
                if n == 0:
                    dve.wait_ge(S["g2_in"], 16)
            for t in range(NT):
                dve.wait_ge(S["x2_sq"], t + 1)
                dve.tensor_scalar(stat[:, 4, t:t + 1], stat[:, 4, t:t + 1], 1.0 / D, EPS, ALU.mult, ALU.add)\
                   .then_inc(S["x2_stat"], 1)
                dve.wait_ge(S["x2_rstd"], t + 1)
                dve.scalar_tensor_tensor(out=xn2[:, t, :], in0=x_rows[:, t, :], scalar=stat[:, 5, t:t + 1],
                                         in1=g2_rows[:, :], op0=ALU.mult, op1=ALU.mult)\
                   .then_inc(S["xn2_done"], 1)
            for r in range(AHEAD):
                if not on_pool(r):
                    split_lo(dve, B_EXP + r)

            def row(n, *shape):
                size = 1
                for x in shape:
                    size *= x
                flat = route[:, n:n + 2, :].rearrange("p a b -> p (a b)")[:, 0:size] if size > NT * NE \
                    else route[:, n, 0:size]
                if len(shape) == 2:
                    return flat.rearrange("p (a b) -> p a b", a=shape[0])
                if len(shape) == 3:
                    return flat.rearrange("p (a b c) -> p a b c", a=shape[0], b=shape[1])
                return flat

            def spread(x, *shape):
                return x.unsqueeze(2).to_broadcast([P, *shape])

            def first_of(dst, x, best, weight, scratch, top, n):
                link(dve.tensor_tensor(scratch, x, spread(best, NT, n), ALU.is_equal))
                link(dve.tensor_tensor(scratch, scratch, weight, ALU.mult))
                link(dve.tensor_reduce(top, scratch, AX.X, ALU.max))
                link(dve.tensor_tensor(dst, scratch, spread(top, NT, n), ALU.is_equal))

            def four(n):
                return route[:, 2, NT * n:NT * (n + 1)]

            falling4, falling16 = row(20, NT, NG), row(21, NT, NE)
            tile_start, count8, count16 = row(22, NE), row(23, 8), row(24, NE)
            zeros16 = row(25, NE)
            link(dve.memset(zeros16, 0.0))
            both = row(0, NT, NG + NE)
            dve.wait_ge(S["consts_pool"], 8)
            dve.wait_ge(S["logits_ps"], NT)
            link(dve.tensor_tensor(both, ps[:, 0, 0:NT * 32].rearrange("p (t n) -> p t n", n=32)[:, :, 0:NG + NE],
                                   router_b[:, :].unsqueeze(1).to_broadcast([P, NT, NG + NE]), ALU.add))
            g_log = both[:, :, 0:NG]
            g_max, g_top, g_sum, e_max, e_top, e_max2, e_sum, scale_t, s_first, s_second = (
                four(n) for n in range(10))
            link(dve.tensor_reduce(g_max, g_log, AX.X, ALU.max))
            dve.tensor_tensor(row(3, NT, NG), g_log, spread(g_max, NT, NG), ALU.subtract)\
               .then_inc(S["gexp_in"], 1)
            g_sel = row(6, NT, NG)
            first_of(g_sel, g_log, g_max, falling4, row(5, NT, NG), g_top, NG)
            link(dve.tensor_scalar(g_sel, g_sel, -1.0, -NEG, ALU.add, ALU.mult))
            e_log = row(7, NT, NE)
            link(dve.tensor_tensor(row(7, NT, NG, EPG),
                                   both[:, :, NG:].rearrange("p t (g e) -> p t g e", g=NG),
                                   g_sel.unsqueeze(3).to_broadcast([P, NT, NG, EPG]), ALU.add))
            link(dve.tensor_reduce(e_max, e_log, AX.X, ALU.max))
            dve.tensor_tensor(row(11, NT, NE), e_log, spread(e_max, NT, NE), ALU.subtract)\
               .then_inc(S["gexp_in"], 1)
            sel1, sel2 = row(8, NT, NE), row(9, NT, NE)
            first_of(sel1, e_log, e_max, falling16, row(10, NT, NE), e_top, NE)
            link(dve.scalar_tensor_tensor(out=e_log, in0=sel1, scalar=NEG, in1=e_log, op0=ALU.mult, op1=ALU.add))
            link(dve.tensor_reduce(e_max2, e_log, AX.X, ALU.max))
            first_of(sel2, e_log, e_max2, falling16, row(10, NT, NE), e_top, NE)
            link(dve.tensor_tensor(sel1, sel1, sel2, ALU.add))
            dve.tensor_copy(picked_bf[:, :, :], sel1).then_inc(S["picked"], 1)
            comb = row(12, NT, NE)
            dve.wait_ge(S["eexp_done"], 1)
            link(dve.tensor_tensor(comb, comb, sel1, ALU.mult))
            link(dve.tensor_reduce(e_sum, comb, AX.X, ALU.add))
            dve.wait_ge(S["gexp_done"], 1)
            link(dve.tensor_reduce(g_sum, row(4, NT, NG), AX.X, ALU.add))
            link(dve.tensor_tensor(scale_t, g_sum, e_sum, ALU.mult))
            link(dve.reciprocal(scale_t, scale_t))
            link(dve.tensor_tensor(comb, comb, spread(scale_t, NT, NE), ALU.mult))
            more, upto, base = row(13, NE), row(14, NE), row(15, NE)
            dve.wait_ge(S["counts_ps"], 1)
            total = ps[:, 1, NT * NE:(NT + 1) * NE]
            link(dve.tensor_scalar(more, total, float(P), None, ALU.is_gt))
            for n in range(2, NT):
                link(dve.scalar_tensor_tensor(out=more, in0=total, scalar=float(n * P), in1=more,
                                              op0=ALU.is_gt, op1=ALU.add))
            link(dve.tensor_tensor_scan(out=upto, data0=more, data1=zeros16, initial=0.0,
                                        op0=ALU.add, op1=ALU.add))
            link(dve.tensor_tensor(base, upto, more, ALU.subtract))
            link(dve.tensor_scalar(base, base, float(P), float((NE - 1) * P), ALU.mult, ALU.add))
            link(dve.tensor_tensor(base, base, tile_start, ALU.subtract))
            slot, late = row(16, NT, NE), row(17, NT, NE)
            before = ps[:, 1, 0:NT * NE].rearrange("p (t n) -> p t n", n=NE)
            link(dve.tensor_scalar(late, before, float(P), None, ALU.is_ge))
            link(dve.tensor_tensor(late, late, base.unsqueeze(1).to_broadcast([P, NT, NE]), ALU.mult))
            link(dve.tensor_tensor(slot, before, tile_start.unsqueeze(1).to_broadcast([P, NT, NE]), ALU.add))
            link(dve.tensor_tensor(slot, slot, late, ALU.add))
            far = float(2 * SLOT_TILES * P)
            link(dve.scalar_tensor_tensor(out=late, in0=slot, scalar=-far, in1=sel1, op0=ALU.add, op1=ALU.mult))
            link(dve.tensor_reduce(s_first, late, AX.X, ALU.min))
            link(dve.tensor_scalar(s_first, s_first, far, None, ALU.add))
            link(dve.tensor_tensor(late, slot, sel1, ALU.mult))
            link(dve.tensor_reduce(s_second, late, AX.X, ALU.max))
            idx = slot_idx[:, :].rearrange("p (t k) -> p t k", k=2)
            dve.tensor_copy(idx[:, :, 0:1], s_first.unsqueeze(2))
            dve.tensor_copy(idx[:, :, 1:2], s_second.unsqueeze(2)).then_inc(S["routed"], 1)
            link(dve.tensor_scalar(late[:, 0, 0:1], upto[:, NE - 1:NE], float(NE), None, ALU.add))
            dve.tensor_copy(tile_table[:, 0:1], late[:, 0, 0:1])
            dve.tensor_copy(tile_table[:, 1:NE + 1], count16)
            over = row(18, 8, NE)
            link(dve.tensor_tensor(over, upto.unsqueeze(1).to_broadcast([P, 8, NE]),
                                   count8.unsqueeze(2).to_broadcast([P, 8, NE]), ALU.is_le))
            link(dve.tensor_reduce(row(3, 8), over, AX.X, ALU.add))
            link(dve.tensor_scalar(row(3, 8), row(3, 8), float(NE - 1), None, ALU.min))
            dve.tensor_copy(tile_table[:, NE + 1:NE + 9], row(3, 8)).then_inc(S["tab"], 1)
            for k, s in enumerate((s_first, s_second)):
                link(dve.tensor_tensor(late, slot, spread(s, NT, NE), ALU.is_equal))
                link(dve.tensor_tensor(late, late, comb, ALU.mult))
                link(dve.tensor_reduce(w_first[:, k, :], late, AX.X, ALU.add))

            def xT_lo_part(n):
                dve.wait_ge(S["xT_hi_done"], n)
                dve.tensor_tensor(xT_lo[:, :, :].rearrange("p k n -> p (k n)"),
                                  ps[:, 3:5, :].rearrange("p a n -> p (a n)"),
                                  xT_hi[:, :, :].rearrange("p k n -> p (k n)").bitcast(F32), ALU.subtract)\
                   .then_inc(S["xT_done"], 1)

            def hT_lo_part(n):
                dve.wait_ge(S["hT_hi_done"], n)
                dve.tensor_tensor(hT_lo[:, :, :].rearrange("p k n -> p (k n)"), ps[:, 2, :],
                                  hT_hi[:, :, :].rearrange("p k n -> p (k n)").bitcast(F32), ALU.subtract)\
                   .then_inc(S["hT_done"], 1)

            def hidden(used, n):
                dve.wait_ge(S["w_used"], used)
                dve.wait_ge(S["silu_done"], n)
                dve.tensor_tensor(hid[:, :], silu[:, :], ps[:, 1, :], ALU.mult).then_inc(S["hid_done"], 1)

            xT_lo_part(1)
            for r in range(AHEAD, 8):
                if not on_pool(r):
                    split_lo(dve, B_EXP + r)
            for r in range(8, 8 + AHEAD):
                if not on_pool(r):
                    split_lo_loop(dve, 1, r - 8)
            hidden(B_EXP + 8, 1)
            xT_lo_part(2)
            tiles = dve.value_load(tile_table[0:1, 0:1], min_val=NE, max_val=MAX_TILES)
            with dve.Fori(1, tiles) as i:
                for r in range(PER_TILE):
                    if not on_pool(8 + r + AHEAD):
                        split_lo_loop(dve, i, r + AHEAD)
                    if r == 5:
                        hT_lo_part(i)
                    if r == 8:
                        dve.wait_ge(S["hT_ps"], i)
                        hidden(loop_block(i, 8), i + 1)
                    if r == 9:
                        xT_lo_part(i + 2)
                dve.wait_ge(S["w_used"], loop_block(i, PER_TILE))
                dve.wait_ge(S["y_stored"], i * 16)
                dve.tensor_copy(y_tile[:, 512:1024], ps[:, 6, :]).then_inc(S["y_dve"], 1)
            hT_lo_part(tiles)
            if not on_pool(8 + AHEAD):
                split_lo_loop(dve, tiles, AHEAD)
            dve.wait_ge(S["w_used"], loop_block(tiles, 4))
            dve.wait_ge(S["y_stored"], tiles * 16)
            dve.tensor_copy(y_tile[:, 512:1024], ps[:, 6, :]).then_inc(S["y_dve"], 1)

            for t in range(NT):
                dve.wait_ge(got_in[t], 32)
                dve.scalar_tensor_tensor(out=y_lo(t), in0=y_lo(t), scalar=w_first[:, 0, t:t + 1],
                                         in1=x_rows[:, t, :], op0=ALU.mult, op1=ALU.add)\
                   .then_inc(S["y_sum"], 1)
                dve.wait_ge(S["y_sum"], 2 * t + 1)
                dve.scalar_tensor_tensor(out=y_lo(t), in0=y_hi(t), scalar=w_first[:, 1, t:t + 1],
                                         in1=y_lo(t), op0=ALU.mult, op1=ALU.add).then_inc(S["y_sum"], 1)
            for t in range(NT):
                dve.wait_ge(S["y_sq"], t + 1)
                dve.tensor_scalar(stat[:, 6, t:t + 1], stat[:, 6, t:t + 1], 1.0 / D, EPS, ALU.mult, ALU.add)\
                   .then_inc(S["y_stat"], 1)
                dve.wait_ge(S["y_rstd"], t + 1)
                dve.scalar_tensor_tensor(out=y_lo(t), in0=y_lo(t), scalar=stat[:, 7, t:t + 1],
                                         in1=gf_rows[:, :], op0=ALU.mult, op1=ALU.mult)\
                   .then_inc(S["y_norm"], 1)


_INS = ("x", "norm1_g", "w_in", "b_gate", "rel_bias", "sgu_norm_g", "sgu_w", "sgu_b", "conv_w", "conv_b",
        "rg_wa", "rg_ba", "rg_wx", "rg_bx", "rg_lambda", "w_branch", "w_out", "norm2_g", "router_grp_w",
        "router_grp_b", "router_exp_w", "router_exp_b", "exp_w_gate", "exp_w_up", "exp_w_down", "final_norm_g")


def kernel(**inputs):
    import numpy as np
    import concourse.bacc as bacc
    from concourse.bass_utils import run_bass_kernel_spmd

    nc = bacc.Bacc("TRN2", target_bir_lowering=False, num_devices=1)
    arrays, args = {}, {}
    for name in _INS:
        x = np.ascontiguousarray(inputs[name])
        arrays[f"in_{name}"] = x
        args[name] = nc.dram_tensor(f"in_{name}", x.shape, mybir.dt.from_np(x.dtype), kind="ExternalInput").ap()
    out = nc.dram_tensor("out", (1, TOK, D), F32, kind="ExternalOutput").ap()
    build(nc, args, out)
    r = run_bass_kernel_spmd(nc, [arrays], core_ids=[0])
    return r.results[0]["out"]
```

```python
from collections import namedtuple
from contextlib import ExitStack

import concourse.bass as bass
from concourse import mybir

F32 = mybir.dt.float32
F32R = mybir.dt.float32r
BF16 = mybir.dt.bfloat16
I32 = mybir.dt.int32
ALU = mybir.AluOpType
ACT = mybir.ActivationFunctionType
AX = mybir.AxisListType

P = 128
TOK = 512
NT = TOK // P
D = 1024
KD = D // P
AW = 512
HEADS = 8
DH = AW // HEADS
CHUNK = 64
NPAIR = AW // P
CLIP = 128
LRU_C = 8.0
CONV = 4
NG = 4
EPG = 4
NE = NG * EPG
DE = D // 2
EPS = 1e-6
NEG = -1e30

Q0, K0, V0, U0, SV0, XG0, XR0, GL0 = (AW * i for i in range(8))

HI_SLOTS = 4
RAW_MIX = 4
AHEAD = 3
PER_PAIR = 5
PER_OUT = 9
B_SV = 0
B_V = 4
B_PAIR = 8
B_GATE = B_PAIR + PER_PAIR * NPAIR
B_OUT = B_GATE + PER_OUT * NPAIR
B_EXP = B_OUT + 8
PER_TILE = 12
PAIRED = 14
XR, KK, QQ, UU, XG = range(PER_PAIR)
BRANCH_ORDER = (2, 1, 0)

PAR_LAM, PAR_CB, PAR_BA, PAR_BX, PAR_CW, PAR_GATE = (NPAIR * n for n in (0, 1, 2, 3, 4, 8))
N_PAR = PAR_GATE + 3 * KD

OVER = 7
MAX_TILES = NE + OVER
SLOT_TILES = MAX_TILES + 1


def on_pool(r):
    return r < 4 or r % 3 == 1


LO_DVE_0 = 32


def pool_before(r):
    return sum(on_pool(x) for x in range(r))


def build(nc, a, out):
    slots = nc.dram_tensor("slots", [SLOT_TILES * P, D], F32, kind="Internal").ap()
    toep = nc.dram_tensor("toep", [HEADS, P, 3 * P], F32, kind="Internal").ap()

    w_in = a["w_in"][0]
    w_branch = a["w_branch"][0]
    w_out = a["w_out"][0]
    w_g, w_u, w_d = a["exp_w_gate"][0], a["exp_w_up"][0], a["exp_w_down"][0]

    ctx = ExitStack()
    with ctx:
        def sem(name):
            return ctx.enter_context(nc.semaphore(name))

        def psum(name, shape, dt=F32):
            return ctx.enter_context(nc.psum_tensor(name, shape, dt))

        def sb(stack, name, shape, dt=F32):
            return stack.enter_context(nc.sbuf_tensor(name, shape, dt))

        raw = sb(ctx, "raw", [P, 6, 1024])
        w_hi = sb(ctx, "w_hi", [P, HI_SLOTS, 1024], F32R)
        w_lo = sb(ctx, "w_lo", [P, HI_SLOTS, 1024], F32R)
        ident = sb(ctx, "ident", [P, P])
        tile_table = sb(ctx, "tile_table", [P, 32], I32)
        stat = sb(ctx, "stat", [P, 8, NT])
        minus_half = sb(ctx, "minus_half", [P, 1])
        w_first = sb(ctx, "w_first", [P, 2, NT])
        slot_idx = sb(ctx, "slot_idx", [P, 2 * NT], I32)
        par = sb(ctx, "par", [P, N_PAR])
        chan = sb(ctx, "chan", [P, 8, NPAIR])
        att = sb(ctx, "att", [P, 3, 4])
        probs_third = sb(ctx, "probs_third", [P, TOK])
        macc = sb(ctx, "macc", [P, 2, TOK])

        AREA_A, AREA_B = 30 * 256, 34 * 256

        with ExitStack() as s0:
            sb(s0, "pad_a0", [P, AREA_A + AREA_B])
            x0 = sb(s0, "x0", [P, NT, D])
            x0_sq = sb(s0, "x0_sq", [P, D])
            g1_rows = sb(s0, "g1_rows", [P, D])

        with ExitStack() as s1:
            v_rows = sb(s1, "v_rows", [P, NT, AW])
            bias = sb(s1, "bias", [P, HEADS, 2 * P])
            qT = sb(s1, "qT", [P, 2, TOK])
            kT = sb(s1, "kT", [P, 2, TOK])
            probs = sb(s1, "probs", [P, 2, TOK])
            probsT = sb(s1, "probsT", [P, TOK])
            sv_rows = sb(s1, "sv_rows", [P, NT, AW])
            sgu_wT = sb(s1, "sgu_wT", [P, 4, P])
            sgu_b_sb = sb(s1, "sgu_b_sb", [P, 4, P])
            sgu_g_sb = sb(s1, "sgu_g_sb", [P, AW])
            wa_diag = sb(s1, "wa_diag", [P, NPAIR, P])
            wx_diag = sb(s1, "wx_diag", [P, NPAIR, P])
            xrT = sb(s1, "xrT", [P, CONV - 1 + TOK])
            conv = sb(s1, "conv", [P, TOK])
            rgate = sb(s1, "rgate", [P, TOK])
            igate = sb(s1, "igate", [P, TOK])
            decay = sb(s1, "decay", [P, TOK])
            gx = sb(s1, "gx", [P, TOK])
            gu = sb(s1, "gu", [P, TOK])
            sb(s1, "pad_b1", [P, AREA_B - (NT * AW + 4 * P + 4 * P + AW + 2 * NPAIR * P + CONV - 1 + 7 * TOK)])
            br_hi = sb(s1, "br_hi", [P, 3, NPAIR, TOK], F32R)
            br_lo = sb(s1, "br_lo", [P, 3, NPAIR, TOK], F32R)
            xn_hi = sb(s1, "xn_hi", [P, KD, TOK], F32R)
            xn_lo = sb(s1, "xn_lo", [P, KD, TOK], F32R)

        with ExitStack() as s2:
            x_rows = sb(s2, "x_rows", [P, NT, D])
            raw_a = sb(s2, "raw_a", [P, 3, 1024])
            sb(s2, "pad_a2", [P, AREA_A - NT * D - 3 * 1024])
            mg_hi = sb(s2, "mg_hi", [P, KD, TOK], F32R)
            mg_lo = sb(s2, "mg_lo", [P, KD, TOK], F32R)
            sb(s2, "pad_b2", [P, AREA_B - 2 * KD * TOK])
            xn2 = sb(s2, "xn2", [P, NT, D])
            g2_rows = sb(s2, "g2_rows", [P, D])
            gf_rows = sb(s2, "gf_rows", [P, D])
            xn2T = sb(s2, "xn2T", [P, 2, D])
            route = sb(s2, "route", [P, 26, NT * NE])
            tri = sb(s2, "tri", [P, 2, P], BF16)
            picked_bf = sb(s2, "picked_bf", [P, NT, NE], BF16)
            router_w = sb(s2, "router_w", [P, KD, NG + NE])
            router_b = sb(s2, "router_b", [P, NG + NE])
            xT_hi = sb(s2, "xT_hi", [P, KD, P], F32R)
            xT_lo = sb(s2, "xT_lo", [P, KD, P], F32R)
            hT_hi = sb(s2, "hT_hi", [P, DE // P, P], F32R)
            hT_lo = sb(s2, "hT_lo", [P, DE // P, P], F32R)
            silu = sb(s2, "silu", [P, DE])
            hid = sb(s2, "hid", [P, DE])
            y_tile = sb(s2, "y_tile", [P, D])
            raw_c = sb(s2, "raw_c", [P, 4, 1024])
        with ExitStack() as s3:
            sb(s3, "pad_a3", [P, AREA_A])
            raw_mg = sb(s3, "raw_mg", [P, 8, 1024])

        gate_buf = raw[:, 4:6, :].rearrange("p a (b n) -> p (a b) n", n=TOK)

        def turned_x(t):
            return ps[:, 2 * t:2 * t + 2, :].rearrange("p a (b n) -> p (a b) n", n=P)

        def macc_of(k):
            return gate_buf[:, 3, :] if k % 2 == 0 else macc[:, 0, :]

        def probs_of(n):
            return probs_third[:, :] if n % 3 == 2 else probs[:, n % 3, :]

        def y_lo(t):
            return raw_mg[:, t, :]

        def y_hi(t):
            return raw_mg[:, 4 + t, :] if t < 3 else raw[:, 0, :]

        ps = psum("ps", [P, 8, 512])

        S = {n: sem(n) for n in (
            "x0_sq_done x0_stat x0_rstd x0_norm x0_turned xn_hi_done xn_done "
            "hi_act lo_pool lo_dve w_used taken "
            "ident_done consts_pool consts_dve zero_done zeros_stored "
            "g1_in chan_in diag_in sgu_in relb_in toep_rev toep_out bias_in bias_done route_in g2_in "
            "sgu_raw sguT_ps sguT_done mask_done sv_sq sv_stat sv_rstd sv_done sp_exp sp_done halved "
            "conv_done gates_ps gates_done "
            "decay_done mult_in mult_done u_done c_mid b_mid ch bh c_ready b_ready mix_ps "
            "scores_ps biased exped normed probsT_ps probsT_done out_ps a_hi a_ready "
            "gate_ready wb_taken macc_done mg_hi_done mg_done x_again x2_ps x2_done x2_sq x2_stat x2_rstd xn2_done "
            "tile0_where xn2T_ps xn2T_done logits_ps gexp_in gexp_done eexp_done picked counts_ps routed scattered tab "
            "x_even_in x_odd_in xT_ps xT_hi_done xT_done silu_done hid_done hT_ps hT_hi_done hT_done "
            "y_act y_dve y_even_stored y_odd_stored y_last_stored before_last_stored all_stored "
            "y_sum y_sq y_stat y_rstd y_norm y_out dve_chain").split()}
        raw_in = [sem(f"raw_in{s}") for s in range(RAW_MIX)]
        even_in = [sem(f"even_in{s}") for s in range(PER_TILE)]
        odd_in = [sem(f"odd_in{s}") for s in range(PER_TILE)]
        x0_in = [sem(f"x0_in{s}") for s in range(NT)]
        got_in = [[sem(f"got{k}_in{t}") for t in range(NT)] for k in range(2)]

        even_buf = ([raw_a[:, n, :] for n in range(3)] + [raw_c[:, n, :] for n in range(4)] + [raw[:, 4, :]]
                    + [raw_mg[:, 7, :], macc[:, :, :].rearrange("p a n -> p (a n)")]
                    + [xn2T[:, n, :] for n in range(2)])
        odd_buf = [raw[:, n, :] for n in (5, 0, 1, 2, 3)] + [raw_mg[:, n, :] for n in range(7)]
        EVEN, ODD = (even_buf, even_in), (odd_buf, odd_in)

        def raw_buf(b):
            return raw[:, b % RAW_MIX, :] if b < B_EXP else even_buf[b - B_EXP]

        def landed(eng, b):
            if b < B_EXP:
                eng.wait_ge(raw_in[b % RAW_MIX], 16 * (b // RAW_MIX + 1))
            else:
                eng.wait_ge(even_in[b - B_EXP], 16)

        x_even, x_odd, y_even, y_odd = (xn2[:, n, :] for n in range(4))
        At = namedtuple("At", "i here here_count then then_count x x_in x_count y y_free y_count")

        def at_even(q):
            return At(2 * q, EVEN, 16 * q + 16, ODD, 16 * q + 16, x_odd, S["x_odd_in"], 16 * q + 16,
                      y_odd, S["y_odd_stored"], 16 * q)

        def at_odd(q):
            return At(2 * q + 1, ODD, 16 * q + 16, EVEN, 16 * q + 32, x_even, S["x_even_in"], 16 * q + 32,
                      y_even, S["y_even_stored"], 16 * q + 16)

        def at_last(n):
            count = 16 * (PAIRED // 2)
            return At(n + (PAIRED - 1), EVEN, n * 16 + count, EVEN, n * 16 + (count + 16),
                      x_even, S["x_even_in"], n * 16 + (count + 16), y_tile[:, :], S["y_last_stored"], n * 16)

        def loop_block(i, r):
            return i * PER_TILE + (B_EXP + 8 + r - PER_TILE)

        def place(at, r):
            (bufs, sems), count = (at.here, at.here_count) if r < PER_TILE else (at.then, at.then_count)
            return bufs[r % PER_TILE], sems[r % PER_TILE], count

        POOL_TILE = pool_before(8 + PER_TILE) - pool_before(8)
        DVE_TILE = PER_TILE - POOL_TILE

        def lo_wait(eng, b):
            if b < B_EXP:
                eng.wait_ge(S["lo_pool"], b + 1)
            elif on_pool(b - B_EXP):
                eng.wait_ge(S["lo_pool"], B_EXP + pool_before(b - B_EXP + 1))
            else:
                eng.wait_ge(S["lo_dve"], LO_DVE_0 + b - B_EXP + 1 - pool_before(b - B_EXP + 1))

        def lo_wait_loop(eng, i, r):
            tile = r // PER_TILE
            c = 8 + r % PER_TILE
            if on_pool(c):
                eng.wait_ge(S["lo_pool"], i * POOL_TILE + (B_EXP + pool_before(c + 1) + (tile - 1) * POOL_TILE))
            else:
                eng.wait_ge(S["lo_dve"],
                            i * DVE_TILE + (LO_DVE_0 + c + 1 - pool_before(c + 1) + (tile - 1) * DVE_TILE))

        def split_hi(b):
            landed(nc.scalar, b)
            if b >= HI_SLOTS:
                nc.scalar.wait_ge(S["w_used"], b - HI_SLOTS + 1)
            nc.scalar.activation(w_hi[:, b % HI_SLOTS, :], raw_buf(b), ACT.Copy)\
                .then_inc(S["hi_act"], 1)

        def split_hi_loop(at, r):
            buf, landed_in, count = place(at, r)
            nc.scalar.wait_ge(landed_in, count)
            nc.scalar.wait_ge(S["w_used"], loop_block(at.i, r) - (HI_SLOTS - 1))
            nc.scalar.activation(w_hi[:, (8 + r) % HI_SLOTS, :], buf, ACT.Copy).then_inc(S["hi_act"], 1)

        def split_lo(eng, b):
            eng.wait_ge(S["hi_act"], b + 1)
            eng.tensor_tensor(w_lo[:, b % HI_SLOTS, :], raw_buf(b),
                              w_hi[:, b % HI_SLOTS, :].bitcast(F32), ALU.subtract)\
               .then_inc(S["lo_pool"] if b < B_EXP or on_pool(b - B_EXP) else S["lo_dve"], 1)

        def split_lo_loop(eng, at, r):
            eng.wait_ge(S["hi_act"], loop_block(at.i, r) + 1)
            eng.tensor_tensor(w_lo[:, (8 + r) % HI_SLOTS, :], place(at, r)[0],
                              w_hi[:, (8 + r) % HI_SLOTS, :].bitcast(F32), ALU.subtract)\
               .then_inc(S["lo_pool"] if on_pool(8 + r) else S["lo_dve"], 1)

        def pair_block(j, r):
            return B_PAIR + PER_PAIR * j + r

        def out_block(m, r):
            return B_GATE + PER_OUT * m + r

        block = ctx.enter_context(nc.Block())

        @block.sync
        def _(sp):
            def rows2(w, k0, c0):
                return w[k0 * P:(k0 + 2) * P, c0:c0 + 512].rearrange("(k p) n -> p k n", p=P)

            def load(b, src, n_k):
                if b >= RAW_MIX:
                    lo_wait(sp, b - RAW_MIX)
                sp.dma_start(raw_buf(b).rearrange("p (k n) -> p k n", k=n_k), src).then_inc(raw_in[b % RAW_MIX], 16)

            def load_block(places, r, src):
                bufs, sems = places
                sp.dma_start(bufs[r].rearrange("p (k n) -> p k n", k=2), src).then_inc(sems[r], 16)

            def tile_source(e, before, r):
                if r < 4:
                    return rows2(w_g[e], 2 * r, 0)
                if r < 8:
                    return rows2(w_u[e], 2 * (r - 4), 0)
                return rows2(w_d[before], 2 * (r % 2), 512 * ((r - 8) // 2))

            for t in range(NT):
                sp.dma_start(x0[:, t, :], a["x"][0, t * P:(t + 1) * P, :]).then_inc(x0_in[t], 16)
            for kp in range(4):
                load(B_SV + kp, rows2(w_in, 2 * kp, SV0), 2)
            sp.dma_start(sgu_g_sb[:, :], a["sgu_norm_g"][0:1, :].broadcast_to([P, AW])).then_inc(S["sgu_in"], 16)
            sp.dma_start(sgu_b_sb[:, :, :].rearrange("p g t -> p (g t)"),
                          a["sgu_b"].rearrange("a g t -> a (g t)").broadcast_to([P, 4 * P]))\
              .then_inc(S["sgu_in"], 16)
            sp.dma_start(gu[:, :].rearrange("t (g s) -> t g s", g=4), a["sgu_w"][0].rearrange("g t s -> t g s"))\
              .then_inc(S["sgu_raw"], 16)
            for r, src in ((PAR_LAM, a["rg_lambda"]), (PAR_CB, a["conv_b"]), (PAR_BA, a["rg_ba"]),
                           (PAR_BX, a["rg_bx"]), (PAR_CW, a["conv_w"][0]), (PAR_GATE, a["b_gate"][0])):
                n = src.shape[0] * src.shape[1] // P
                sp.dma_start(gx[r:r + n, 0:P], src.rearrange("a (c p) -> (a c) p", p=P)).then_inc(S["chan_in"], 16)
            sp.wait_ge(S["consts_dve"], 2)
            for w, dst in (("rg_wa", wa_diag), ("rg_wx", wx_diag)):
                for h in range(2):
                    sp.dma_start(dst[h * 64:(h + 1) * 64, :, h * 64:(h + 1) * 64],
                                  a[w][0].rearrange("(c h) i j -> h i c j", h=2)[h]).then_inc(S["diag_in"], 16)
            for kp in range(4):
                load(B_V + kp, rows2(w_in, 2 * kp, V0), 2)

            def cols(c0):
                return w_in[:, c0:c0 + P].rearrange("(k p) n -> p k n", p=P)

            sp.wait_ge(S["zero_done"], 1)
            for j in range(NPAIR):
                for r, c0 in enumerate((XR0, K0, Q0, U0, XG0)):
                    load(pair_block(j, r), cols(c0 + j * P), KD)
                for n in range(j * SLOT_TILES // NPAIR, (j + 1) * SLOT_TILES // NPAIR):
                    sp.dma_start(slots[n * P:(n + 1) * P, :], raw[:, 4, :]).then_inc(S["zeros_stored"], 16)
            for m in range(NPAIR):
                if m == 2:
                    sp.wait_ge(S["a_ready"], NPAIR)
                    sp.dma_start(x_rows[:, :, :], a["x"][0].rearrange("(t p) n -> p t n", p=P))\
                      .then_inc(S["x_again"], 16)
                for o, br in enumerate(BRANCH_ORDER):
                    for c in range(2):
                        load(out_block(m, 3 * o + c), cols(GL0 + br * D + (2 * m + c) * P), KD)
                    load(out_block(m, 3 * o + 2),
                         w_branch[br, :, 2 * m * P:2 * (m + 1) * P].rearrange("(k p) n -> p k n", p=P), 4)
            for n in range(2):
                for kp in range(4):
                    load(B_OUT + 4 * n + kp, rows2(w_out, 2 * kp, 512 * n), 2)
            sp.wait_ge(S["a_ready"], NPAIR)
            for r in range(8):
                if r == 3:
                    sp.wait_ge(S["w_used"], B_OUT)
                if r == 7:
                    sp.wait_ge(S["mg_done"], KD)
                load_block(EVEN, r, tile_source(0, 0, r))
            for r in range(PER_TILE):
                if 1 <= r <= RAW_MIX:
                    lo_wait(sp, B_EXP - RAW_MIX + r - 1)
                if r == RAW_MIX + 1:
                    sp.wait_ge(S["w_used"], B_EXP)
                load_block(ODD, r, tile_source(1, 0, r))
            for r in range(8, PER_TILE):
                sp.sem_inc(even_in[r], 16)
            sp.wait_ge(S["logits_ps"], NT)

            def load_rows(k, dst, landed_in, turned):
                sp.wait_ge(S["xT_ps"], turned)
                sp.dma_start(dst, slots[bass.ds(k * P, P), :]).then_inc(landed_in, 16)

            def rows_after(i, places):
                if places is EVEN:
                    load_rows(i + 1, x_odd, S["x_odd_in"], i)
                else:
                    load_rows(i + 1, x_even, S["x_even_in"], i)

            def load_tile(i, places, tiles_back, e, before):
                for r in range(PER_TILE):
                    if r == 8:
                        if tiles_back == 1 or isinstance(i, int) and i >= PAIRED:
                            load_rows(i + 1, x_even, S["x_even_in"], i + 1)
                        else:
                            rows_after(i, places)
                    lo_wait_loop(sp, i, r - tiles_back * PER_TILE)
                    load_block(places, r, tile_source(e, before, r))

            sp.sem_inc(S["x_even_in"], 16)
            for r in range(PER_TILE):
                if r == 3:
                    sp.wait_ge(S["scattered"], 16 * 2 * NT)
                    load_rows(1, x_odd, S["x_odd_in"], 1)
                    load_rows(2, x_even, S["x_even_in"], 1)
                if r == 8:
                    rows_after(2, EVEN)
                if r < 8:
                    lo_wait(sp, B_EXP + r)
                load_block(EVEN, r, tile_source(2, 1, r))
            load_tile(3, ODD, 2, 3, 2)
            with sp.Fori(2, PAIRED // 2) as q:
                load_tile(2 * q, EVEN, 2, 2 * q, 2 * q - 1)
                load_tile(2 * q + 1, ODD, 2, 2 * q + 1, 2 * q)
            load_tile(PAIRED, EVEN, 2, PAIRED, PAIRED - 1)
            sp.wait_ge(S["tab"], 1)
            n_last = sp.value_load(tile_table[0:1, 0:1], min_val=NE - PAIRED + 1, max_val=MAX_TILES - PAIRED + 1)
            with sp.Fori(2, n_last) as n:
                e = sp.value_load(tile_table[0:1, bass.ds(n + PAIRED, 1)], min_val=0, max_val=NE - 1)
                before = sp.value_load(tile_table[0:1, bass.ds(n + (PAIRED - 1), 1)], min_val=0, max_val=NE - 1)
                load_tile(n + (PAIRED - 1), EVEN, 1, e, before)
            last = sp.value_load(tile_table[0:1, bass.ds(n_last + (PAIRED - 1), 1)], min_val=0, max_val=NE - 1)
            for r in range(4):
                lo_wait_loop(sp, n_last + (PAIRED - 1), r - PER_TILE)
                load_block(EVEN, r, tile_source(last, last, 8 + r))

            for t in range(NT):
                sp.wait_ge(S["y_norm"], t + 1)
                sp.dma_start(out[0, t * P:(t + 1) * P, :], y_lo(t)).then_inc(S["y_out"], 16)
            sp.wait_ge(S["y_out"], 16 * NT)

        @block.gpsimd
        def _(pool):
            pool.memset(ident[:, :], 0.0).then_inc(S["ident_done"], 1)
            pool.memset(minus_half[:, :], -0.5).then_inc(S["consts_pool"], 1)
            pool.wait_ge(S["ident_done"], 1)
            pool.affine_select(out=ident[:, :], in_=ident[:, :], compare_op=ALU.not_equal, fill=1.0, base=0,
                               pattern=[[-1, P]], channel_multiplier=1).then_inc(S["ident_done"], 1)
            pool.wait_ge(S["consts_pool"], 1)
            for t in range(NT):
                pool.wait_ge(S["x0_stat"], t + 1)
                pool.tensor_tensor(stat[:, 1, t:t + 1], stat[:, 0, t:t + 1], minus_half[:, :], ALU.pow)\
                    .then_inc(S["x0_rstd"], 1)
            for b in range(AHEAD):
                split_lo(pool, b)
            pool.wait_ge(S["toep_rev"], 2)
            pool.dma_start(toep, probs[0:HEADS, 0, 0:3 * P].unsqueeze(1).to_broadcast([HEADS, P, 3 * P])).then_inc(S["toep_out"], 16)
            pool.wait_ge(S["toep_out"], 16)
            pool.dma_start(bias[:, :, :], bass.AP(toep.tensor, P - 1, [[3 * P - 1, P], [3 * P * P, HEADS], [1, 2 * P]]))\
                .then_inc(S["bias_in"], 16)
            pool.memset(gate_buf[:, 0:2, :], 0.0).then_inc(S["zero_done"], 1)
            for b in range(AHEAD, B_PAIR + AHEAD):
                split_lo(pool, b)
                if b == AHEAD + 1:
                    pool.wait_ge(S["bias_in"], 16)
                    pool.memset(bias[0:CHUNK, :, 3 * CHUNK:4 * CHUNK], NEG).then_inc(S["bias_done"], 1)
                    pool.wait_ge(S["sguT_done"], 1)
                    pool.affine_select(out=sgu_wT[:, :, :], in_=sgu_wT[:, :, :], compare_op=ALU.is_ge, fill=0.0,
                                       base=0, pattern=[[0, 4], [1, P]], channel_multiplier=-1)\
                        .then_inc(S["mask_done"], 1)
            for t in range(NT):
                pool.wait_ge(S["sv_stat"], t + 1)
                pool.tensor_tensor(stat[:, 3, t:t + 1], stat[:, 2, t:t + 1], minus_half[:, :], ALU.pow)\
                    .then_inc(S["sv_rstd"], 1)

            for b in range(B_PAIR, B_OUT):
                split_lo(pool, b + AHEAD)
            for b in range(B_OUT + AHEAD, B_EXP):
                split_lo(pool, b)
            pool.memset(tri[:, :, :], 1.0).then_inc(S["consts_pool"], 1)
            pool.wait_ge(S["consts_pool"], 2)
            pool.affine_select(out=tri[:, 0, :], in_=tri[:, 0, :], compare_op=ALU.is_gt, fill=0.0, base=0,
                               pattern=[[1, P]], channel_multiplier=-1).then_inc(S["consts_pool"], 1)
            for r, (base, pattern) in enumerate((
                    (NG, [[0, NT], [-1, NG]]), (NE, [[0, NT], [-1, NE]]),
                    (0, [[P, NE]]), (0, [[1, 8]]), (0, [[1, NE]]))):
                n = 1
                for _, c in pattern:
                    n *= c
                pool.iota(route[:, 20 + r, 0:n], pattern=pattern, base=base, channel_multiplier=0,
                          allow_small_or_imprecise_dtypes=True)\
                    .then_inc(S["consts_pool"], 1)
            pool.iota(hid[:, 0:P], pattern=[[1, P]], base=0, channel_multiplier=0,
                      allow_small_or_imprecise_dtypes=True).then_inc(S["consts_pool"], 1)
            for t in range(NT):
                pool.wait_ge(S["x2_stat"], t + 1)
                pool.tensor_tensor(stat[:, 5, t:t + 1], stat[:, 4, t:t + 1], minus_half[:, :], ALU.pow)\
                    .then_inc(S["x2_rstd"], 1)
            for r in range(AHEAD):
                split_lo(pool, B_EXP + r)
            pool.wait_ge(S["zeros_stored"], 16 * SLOT_TILES)
            pool.wait_ge(S["xn2_done"], NT)
            pool.wait_ge(S["routed"], 1)
            for t in range(NT):
                for k in range(2):
                    pool.indirect_dma_start(
                        slots, bass.IndirectOffsetOnAxis(ap=slot_idx[:, 2 * t + k:2 * t + k + 1], axis=0),
                        xn2[:, t, :], None).then_inc(S["scattered"], 16)
            for r in range(AHEAD, 8 + AHEAD):
                if r < 8:
                    if on_pool(r):
                        split_lo(pool, B_EXP + r)
            for r in range(8, 8 + AHEAD):
                if on_pool(r):
                    split_lo_loop(pool, at_odd(0), r - 8)
            def tile(at):
                for r in range(PER_TILE):
                    if on_pool(8 + r + AHEAD):
                        split_lo_loop(pool, at, r + AHEAD)

            tile(at_odd(0))
            with pool.Fori(1, PAIRED // 2) as q:
                tile(at_even(q))
                tile(at_odd(q))
            pool.wait_ge(S["tab"], 1)
            n_last = pool.value_load(tile_table[0:1, 0:1], min_val=NE - PAIRED + 1, max_val=MAX_TILES - PAIRED + 1)
            tiles = n_last + (PAIRED - 1)
            with pool.Fori(1, n_last) as n:
                tile(at_last(n))
            if on_pool(8 + AHEAD):
                split_lo_loop(pool, at_last(n_last), AHEAD)
            def gather(k, dst, t):
                pool.indirect_dma_start(
                    dst, None, slots,
                    bass.IndirectOffsetOnAxis(ap=slot_idx[:, 2 * t + k:2 * t + k + 1], axis=0))\
                    .then_inc(got_in[k][t], 16)

            pool.wait_ge(S["before_last_stored"], 1)
            for t in range(NT):
                gather(0, y_lo(t), t)
            pool.wait_ge(S["all_stored"], 1)
            for t in range(NT):
                gather(1, y_hi(t), t)
            for t in range(NT):
                pool.wait_ge(S["y_stat"], t + 1)
                pool.tensor_tensor(stat[:, 7, t:t + 1], stat[:, 6, t:t + 1], minus_half[:, :], ALU.pow)\
                    .then_inc(S["y_rstd"], 1)

        @block.scalar
        def _(act):
            act.dma_start(g1_rows[:, :], a["norm1_g"][0:1, :].broadcast_to([P, D])).then_inc(S["g1_in"], 16)
            act.dma_start(probs[0:HEADS, 1, 0:2 * CLIP + 1], a["rel_bias"][0]).then_inc(S["relb_in"], 16)
            for t in range(NT):
                act.wait_ge(x0_in[t], 16)
                if t > 0:
                    act.wait_ge(S["x0_sq_done"], t)
                act.activation(x0_sq[:, :], x0[:, t, :], ACT.Square, accum_out=stat[:, 0, t:t + 1])\
                   .then_inc(S["x0_sq_done"], 1)
            for t in range(NT):
                if t < AHEAD:
                    split_hi(t)
                act.wait_ge(S["x0_turned"], t + 1)
                act.activation(xn_hi[:, :, t * P:(t + 1) * P], turned_x(t), ACT.Copy)\
                   .then_inc(S["xn_hi_done"], 1)
            act.wait_ge(S["sp_exp"], 1)
            act.activation(chan[:, 1, :], chan[:, 0, :], ACT.Exp, scale=-1.0).then_inc(S["sp_exp"], 1)

            for b in range(B_SV, B_V):
                split_hi(b + AHEAD)
            for b in range(B_V, B_PAIR):
                split_hi(b + AHEAD)
                t = b - B_V
                if t == 0:
                    act.wait_ge(S["w_used"], B_V)
                act.activation(sv_rows[:, t, :], ps[:, t, :], ACT.Gelu_apprx_tanh).then_inc(S["taken"], 1)
            for t in range(NT):
                act.wait_ge(S["taken"], t + 1)
                if t > 0:
                    act.wait_ge(S["sv_sq"], t)
                else:
                    act.wait_ge(S["sguT_done"], 1)
                act.activation(gx[:, :], sv_rows[:, t, :], ACT.Square, accum_out=stat[:, 2, t:t + 1])\
                   .then_inc(S["sv_sq"], 1)
            act.wait_ge(S["w_used"], B_PAIR)
            for t in range(NT):
                act.activation(v_rows[:, t, :], ps[:, 4 + t, :], ACT.Copy).then_inc(S["taken"], 1)

            def exps(n):
                w = P * (n % NT + 1)
                act.wait_ge(S["biased"], n + 1)
                act.activation(probs_of(n)[:, 0:w], probs_of(n)[:, 0:w], ACT.Exp, bias=att[:, n % 3, 0:1],
                               accum_out=att[:, n % 3, 1:2]).then_inc(S["exped"], 1)

            def take_probsT(n):
                w = P * (n % NT + 1)
                act.wait_ge(S["probsT_ps"], n + 1)
                if n >= 1:
                    act.wait_ge(S["out_ps"], n)
                act.activation(probsT[:, 0:w], ps[:, 6, 0:w], ACT.Copy).then_inc(S["probsT_done"], 1)

            def attention(jp, u):
                if 4 <= u < 12:
                    take_probsT(8 * jp + u - 4)
                if 1 <= u < 9:
                    exps(8 * jp + u - 1)

            def a_out_hi(jp):
                act.wait_ge(S["out_ps"], 8 * (jp + 1))
                act.activation(br_hi[:, 0, jp, :], ps[:, 7, :], ACT.Copy).then_inc(S["a_hi"], 1)

            def take(b, dst, func):
                act.wait_ge(S["w_used"], b + 1)
                act.activation(dst, ps[:, b % 2, :], func).then_inc(S["taken"], 1)

            def c_hi(j):
                act.wait_ge(S["c_mid"], j + 1)
                act.activation(br_hi[:, 2, j, :], gx[:, :], ACT.Copy).then_inc(S["ch"], 1)

            def b_hi(j):
                act.wait_ge(S["b_mid"], j + 1)
                act.activation(br_hi[:, 1, j, :], gu[:, :], ACT.Copy).then_inc(S["bh"], 1)

            for j in range(NPAIR):
                for r in range(PER_PAIR):
                    b = pair_block(j, r)
                    split_hi(b + AHEAD)
                    if r == XR and j > 0:
                        if j > 1:
                            act.wait_ge(S["c_ready"], j - 1)
                        take(b - 1, gx[:, :], ACT.Gelu_apprx_tanh)
                    if r == KK:
                        if j > 0:
                            act.wait_ge(S["conv_done"], j)
                        take(b - 1, xrT[:, CONV - 1:], ACT.Copy)
                    if r == QQ:
                        take(b - 1, kT[:, j % 2, :], ACT.Copy)
                    if r == UU:
                        take(b - 1, qT[:, j % 2, :], ACT.Copy)
                    for n in range(3 * r, 3 * r + 3):
                        if j > 0:
                            attention(j - 1, n)
                    if r == QQ and j > 0:
                        c_hi(j - 1)
                        b_hi(j - 1)
                    if r == UU:
                        if j > 0:
                            a_out_hi(j - 1)
                        act.wait_ge(S["gates_ps"], 2 * j + 2)
                        act.wait_ge(S["halved"], 1)
                        if j > 0:
                            act.wait_ge(S["b_mid"], j)
                        act.activation(rgate[:, :], ps[:, 2, :], ACT.Tanh, scale=0.5,
                                       bias=par[:, PAR_BA + j:PAR_BA + j + 1])\
                           .then_inc(S["gates_done"], 1)
                        act.activation(igate[:, :], ps[:, 3, :], ACT.Tanh, scale=0.5,
                                       bias=par[:, PAR_BX + j:PAR_BX + j + 1])\
                           .then_inc(S["gates_done"], 1)
                        act.wait_ge(S["gates_done"], 2 * j + 1)
                        act.wait_ge(S["sp_done"], 1)
                        act.activation(decay[:, :], rgate[:, :], ACT.Exp, scale=chan[:, 3, j:j + 1],
                                       bias=chan[:, 3, j:j + 1])\
                           .then_inc(S["decay_done"], 1)
                        act.wait_ge(S["decay_done"], 2 * j + 1)
                        act.activation(rgate[:, :], rgate[:, :], ACT.Tanh, scale=chan[:, 2, j:j + 1],
                                       bias=chan[:, 2, j:j + 1])\
                           .then_inc(S["decay_done"], 1)
                    if r == XG:
                        if j > 0:
                            act.wait_ge(S["b_ready"], j)
                        else:
                            act.wait_ge(S["sguT_ps"], 1)
                        take(b - 1, gu[:, :], ACT.Copy)
                        act.wait_ge(S["mult_in"], j + 1)
                        act.activation(rgate[:, :], rgate[:, :], ACT.Sqrt).then_inc(S["mult_done"], 1)
                        act.wait_ge(S["taken"], b)
                        act.activation(gu[:, :], gu[:, :], ACT.Gelu_apprx_tanh).then_inc(S["u_done"], 1)

            def gate(m, o, c):
                g = 6 * m + 2 * o + c
                br = BRANCH_ORDER[o]
                act.wait_ge(S["w_used"], out_block(m, 3 * o + c) + 1)
                if g >= 3:
                    act.wait_ge(S["wb_taken"], g - 2)
                else:
                    act.wait_ge(S["zeros_stored"], 16 * SLOT_TILES)
                act.activation(gate_buf[:, g % 3, :], ps[:, c, :], ACT.Tanh, scale=0.5,
                               bias=par[:, PAR_GATE + KD * br + 2 * m + c:PAR_GATE + KD * br + 2 * m + c + 1]).then_inc(S["gate_ready"], 1)

            def mg_hi_part(k):
                act.wait_ge(S["macc_done"], k + 1)
                act.activation(mg_hi[:, k, :], macc_of(k), ACT.Copy, scale=0.5).then_inc(S["mg_hi_done"], 1)

            for m in range(NPAIR):
                n = 0
                for r in range(PER_OUT):
                    b = out_block(m, r)
                    split_hi(b + AHEAD)
                    if m == 0 and r == 0:
                        act.wait_ge(S["c_ready"], NPAIR - 1)
                        take(b - 1, gx[:, :], ACT.Gelu_apprx_tanh)
                    if r > 0 and (r - 1) % 3 < 2:
                        gate(m, (r - 1) // 3, (r - 1) % 3)
                    if m == 0:
                        for _ in range(2 if r % 3 == 2 else 3):
                            if n < 12:
                                attention(NPAIR - 1, n)
                            n += 1
                        if r == 1:
                            c_hi(NPAIR - 1)
                            b_hi(NPAIR - 1)
                        if r == 5:
                            a_out_hi(NPAIR - 1)
                    if r == 0 and m > 0:
                        for c in range(2):
                            mg_hi_part(2 * (m - 1) + c)
            for b in range(B_OUT + AHEAD, B_EXP):
                split_hi(b)
                if b == B_OUT + AHEAD:
                    for c in range(2):
                        mg_hi_part(KD - 2 + c)
                    act.dma_start(g2_rows[:, :], a["norm2_g"][0:1, :].broadcast_to([P, D])).then_inc(S["g2_in"], 16)
                    act.dma_start(router_w[:, :, 0:NG], a["router_grp_w"][0].rearrange("(k p) n -> p k n", p=P))\
                       .then_inc(S["route_in"], 16)
                    act.dma_start(router_w[:, :, NG:], a["router_exp_w"][0].rearrange("(k p) n -> p k n", p=P))\
                       .then_inc(S["route_in"], 16)
                    act.dma_start(router_b[:, 0:NG], a["router_grp_b"][0:1, :].broadcast_to([P, NG]))\
                       .then_inc(S["route_in"], 16)
                    act.dma_start(router_b[:, NG:], a["router_exp_b"][0:1, :].broadcast_to([P, NE]))\
                       .then_inc(S["route_in"], 16)
                    act.dma_start(gf_rows[:, :],
                                  a["final_norm_g"].rearrange("(a n) -> a n", a=1).broadcast_to([P, D]))\
                       .then_inc(S["route_in"], 16)
            for t in range(NT + 1):
                if t < NT:
                    act.wait_ge(S["x2_done"], NT + t + 1)
                    if t > 0:
                        act.wait_ge(S["x2_sq"], t)
                    act.activation(y_tile[:, :], x_rows[:, t, :], ACT.Square, accum_out=stat[:, 4, t:t + 1])\
                       .then_inc(S["x2_sq"], 1)
                if 1 <= t <= NT:
                    u = t - 1
                    act.wait_ge(S["xn2T_ps"], u + 1)
                    if u >= 2:
                        act.wait_ge(S["logits_ps"], u - 1)
                    act.activation(xn2T[:, u % 2, :], ps[:, 4 + 2 * (u % 2):6 + 2 * (u % 2), :].rearrange(
                        "p a n -> p (a n)"), ACT.Copy).then_inc(S["xn2T_done"], 1)
            for r in range(AHEAD):
                split_hi(B_EXP + r)
            act.wait_ge(S["gexp_in"], 1)
            act.activation(route[:, 4, 0:4 * NG], route[:, 3, 0:4 * NG], ACT.Exp).then_inc(S["gexp_done"], 1)
            act.wait_ge(S["gexp_in"], 2)
            act.activation(route[:, 12, :], route[:, 11, :], ACT.Exp).then_inc(S["eexp_done"], 1)

            def xT_hi_part(n):
                act.wait_ge(S["xT_ps"], n)
                act.activation(xT_hi[:, :, :].rearrange("p k n -> p (k n)"),
                               ps[:, 3:5, :].rearrange("p a n -> p (a n)"), ACT.Copy)\
                   .then_inc(S["xT_hi_done"], 1)

            def silu_part(used):
                act.wait_ge(S["w_used"], used)
                act.activation(silu[:, :], ps[:, 0, :], ACT.Silu).then_inc(S["silu_done"], 1)

            def hT_hi_part(n):
                act.wait_ge(S["hT_ps"], n)
                act.activation(hT_hi[:, :, :].rearrange("p k n -> p (k n)"), ps[:, 2, :], ACT.Copy)\
                   .then_inc(S["hT_hi_done"], 1)

            def y_part(used, at):
                n = at.i
                act.wait_ge(S["w_used"], used)
                act.wait_ge(at.y_free, at.y_count)
                act.activation(at.y[:, 0:512], ps[:, 5, :], ACT.Copy).then_inc(S["y_act"], 1)
                act.wait_ge(S["y_act"], n + 1)
                act.wait_ge(S["y_dve"], n + 1)
                act.dma_start(slots[bass.ds((n - 1) * P, P), :], at.y).then_inc(at.y_free, 16)

            for name in ("y_even_stored", "y_odd_stored", "y_last_stored"):
                act.sem_inc(S[name], 16)
            act.sem_inc(S["y_act"], 1)
            xT_hi_part(1)
            for r in range(8):
                if r + AHEAD < 8:
                    split_hi(B_EXP + r + AHEAD)
                elif r + AHEAD == 8:
                    split_hi_loop(at_odd(0), 0)
                else:
                    split_hi_loop(at_odd(0), r + AHEAD - 8)
                if r == 4:
                    silu_part(B_EXP + 4)
            xT_hi_part(2)
            def tile(at):
                i = at.i
                for r in range(PER_TILE):
                    split_hi_loop(at, r + AHEAD)
                    if r == 4:
                        act.wait_ge(S["hid_done"], i)
                        silu_part(loop_block(i, 4))
                    if r == 5:
                        hT_hi_part(i)
                    if r == 9:
                        xT_hi_part(i + 2)
                y_part(loop_block(i, PER_TILE), at)

            tile(at_odd(0))
            with act.Fori(1, PAIRED // 2) as q:
                tile(at_even(q))
                tile(at_odd(q))
            act.wait_ge(S["tab"], 1)
            n_last = act.value_load(tile_table[0:1, 0:1], min_val=NE - PAIRED + 1, max_val=MAX_TILES - PAIRED + 1)
            tiles = n_last + (PAIRED - 1)
            with act.Fori(1, n_last) as n:
                tile(at_last(n))
            hT_hi_part(tiles)
            split_hi_loop(at_last(n_last), AHEAD)
            act.wait_ge(S["y_even_stored"], 16 * (PAIRED // 2 + 1))
            act.wait_ge(S["y_odd_stored"], 16 * (PAIRED // 2))
            act.wait_ge(S["y_last_stored"], n_last * 16)
            act.sem_inc(S["before_last_stored"], 1)
            y_part(loop_block(tiles, 4), at_last(n_last))
            act.wait_ge(S["y_last_stored"], n_last * 16 + 16)
            act.sem_inc(S["all_stored"], 1)
            for t in range(NT):
                act.wait_ge(S["y_sum"], NT + t + 1)
                if t > 0:
                    act.wait_ge(S["y_sq"], t)
                act.activation(xn2[:, 0, :], y_lo(t), ACT.Square, accum_out=stat[:, 6, t:t + 1])\
                   .then_inc(S["y_sq"], 1)

        @block.tensor
        def _(pe):
            def three(dst, hi_l, lo_l, hi_r, lo_r, start, stop):
                pe.matmul(dst, hi_l, hi_r, start=start, stop=False)
                pe.matmul(dst, hi_l, lo_r, start=False, stop=False)
                return pe.matmul(dst, lo_l, hi_r, start=False, stop=stop)

            def w(b, part):
                return (w_hi, w_lo)[part][:, b % HI_SLOTS, :]

            pe.wait_ge(S["ident_done"], 2)
            for t in range(NT):
                pe.wait_ge(S["x0_norm"], t + 1)
                for k in range(KD):
                    mm = pe.transpose(ps[:, 2 * t + k // 4, (k % 4) * P:(k % 4 + 1) * P], x0[:, t, k * P:(k + 1) * P], ident[:, :])
                mm.then_inc(S["x0_turned"], 1)
            def rows_block(b, kp, lhs_hi, lhs_lo, bank):
                lo_wait(pe, b)
                for t in range(NT):
                    if b == 0:
                        pe.wait_ge(S["xn_done"], t + 1)
                    for kk in range(2):
                        k = 2 * kp + kk
                        mm = three(ps[:, bank + t, :], lhs_hi[:, k, t * P:(t + 1) * P],
                                   lhs_lo[:, k, t * P:(t + 1) * P],
                                   w(b, 0)[:, kk * 512:(kk + 1) * 512], w(b, 1)[:, kk * 512:(kk + 1) * 512],
                                   k == 0, k == KD - 1)
                mm.then_inc(S["w_used"], 1)

            rows_block(B_SV, 0, xn_hi, xn_lo, 0)
            pe.wait_ge(S["chan_in"], 96)
            pe.transpose(ps[:, 6, 0:N_PAR], gx[0:N_PAR, 0:P], ident[0:N_PAR, 0:N_PAR])
            pe.wait_ge(S["sgu_raw"], 16)
            for g in range(4):
                mm = pe.transpose(ps[:, 7, g * P:(g + 1) * P], gu[:, g * P:(g + 1) * P], ident[:, :])
            mm.then_inc(S["sguT_ps"], 1)
            for kp in range(1, 4):
                rows_block(B_SV + kp, kp, xn_hi, xn_lo, 0)
            pe.wait_ge(S["sguT_done"], 1)
            for kp in range(4):
                rows_block(B_V + kp, kp, xn_hi, xn_lo, 4)

            def cols_piece(b, bank, ks):
                for k in ks:
                    mm = three(ps[:, bank, :], w(b, 0)[:, k * P:(k + 1) * P], w(b, 1)[:, k * P:(k + 1) * P],
                               xn_hi[:, k, :], xn_lo[:, k, :], k == 0, k == KD - 1)
                if ks[-1] == KD - 1:
                    mm.then_inc(S["w_used"], 1)

            PIECES = ((0, 1, 2), (3, 4, 5), (6, 7))

            def scores(n):
                jp, u = n // 8, n % 8
                h, i = u // NT, u % NT
                hp = slice(DH * h, DH * (h + 1))
                if n == 0:
                    pe.wait_ge(S["taken"], 8)
                if u == 0:
                    pe.wait_ge(S["taken"], pair_block(jp, QQ) + 1)
                if n >= 2:
                    pe.wait_ge(S["biased"], n - 1)
                pe.matmul(ps[:, 4 + n % 2, 0:(i + 1) * P], qT[hp, jp % 2, i * P:(i + 1) * P],
                          kT[hp, jp % 2, 0:(i + 1) * P], start=True, stop=True).then_inc(S["scores_ps"], 1)

            def turn_probs(n):
                i = n % NT
                pe.wait_ge(S["normed"], n + 1)
                if n >= 1:
                    pe.wait_ge(S["probsT_done"], n)
                for kt in range(i + 1):
                    mm = pe.transpose(ps[:, 6, kt * P:(kt + 1) * P], probs_of(n)[:, kt * P:(kt + 1) * P],
                                      ident[:, :])
                mm.then_inc(S["probsT_ps"], 1)

            def times_v(n):
                jp, u = n // 8, n % 8
                h, i = u // NT, u % NT
                pe.wait_ge(S["probsT_done"], n + 1)
                if u == 0 and jp > 0:
                    pe.wait_ge(S["a_ready"], jp)
                for kt in range(i + 1):
                    mm = pe.matmul(ps[DH * h:DH * (h + 1), 7, i * P:(i + 1) * P],
                                   v_rows[:, kt, (2 * jp + h) * DH:(2 * jp + h + 1) * DH],
                                   probsT[:, kt * P:(kt + 1) * P], start=(kt == 0), stop=(kt == i))
                mm.then_inc(S["out_ps"], 1)

            def attention(jp, u):
                if 4 <= u < 12:
                    times_v(8 * jp + u - 4)
                if 3 <= u < 11:
                    turn_probs(8 * jp + u - 3)
                if u < 8:
                    scores(8 * jp + u)

            for j in range(NPAIR):
                for r in range(PER_PAIR):
                    b = pair_block(j, r)
                    lo_wait(pe, b)
                    pe.wait_ge(S["taken"], b - 1 if b >= B_PAIR + 2 else 4)
                    for piece, ks in enumerate(PIECES):
                        cols_piece(b, b % 2, ks)
                        if j > 0:
                            attention(j - 1, 3 * r + piece)
                        if r == QQ and piece == 2:
                            pe.wait_ge(S["conv_done"], j + 1)
                            pe.wait_ge(S["diag_in"], 64)
                            if j > 0:
                                pe.wait_ge(S["b_mid"], j)
                            pe.matmul(ps[:, 2, :], wa_diag[:, j, :], conv[:, :], start=True, stop=True)\
                              .then_inc(S["gates_ps"], 1)
                            pe.matmul(ps[:, 3, :], wx_diag[:, j, :], conv[:, :], start=True, stop=True)\
                              .then_inc(S["gates_ps"], 1)
                        if r == XG and piece == 0:
                            pe.wait_ge(S["gates_done"], 2 * j + 2)
                            pe.wait_ge(S["sv_done"], NT)
                            pe.wait_ge(S["mask_done"], 1)
                            for n in range(NT):
                                mm = pe.matmul(ps[:, 2, n * P:(n + 1) * P], sv_rows[:, n, j * P:(j + 1) * P],
                                               sgu_wT[:, j, :], start=True, stop=True)
                            mm.then_inc(S["mix_ps"], 1)

            for m in range(NPAIR):
                n = 0
                for r in range(PER_OUT):
                    b = out_block(m, r)
                    o, c = r // 3, r % 3
                    br = BRANCH_ORDER[o]
                    lo_wait(pe, b)
                    if c < 2:
                        g = 6 * m + 2 * o + c
                        if g < 2:
                            pe.wait_ge(S["taken"], B_GATE - 1 + c)
                        else:
                            pe.wait_ge(S["gate_ready"], g - 1)
                        for ks in PIECES:
                            cols_piece(b, c, ks)
                            if m == 0 and n < 12:
                                attention(NPAIR - 1, n)
                            n += 1
                    else:
                        pe.wait_ge(S[("a_ready", "b_ready", "c_ready")[br]], NPAIR)
                        for c in range(2):
                            g = 6 * m + 2 * o + c
                            if g >= 2:
                                pe.wait_ge(S["wb_taken"], g - 1)
                            else:
                                pe.wait_ge(S["b_mid"], NPAIR)
                            for k in range(NPAIR):
                                at = k * 2 * P + c * P
                                mm = three(ps[:, 2 + c, :], w(b, 0)[:, at:at + P], w(b, 1)[:, at:at + P],
                                           br_hi[:, br, k, :], br_lo[:, br, k, :], k == 0, k == NPAIR - 1)
                            if c == 1:
                                mm.then_inc(S["w_used"], 1)
                            if m == 0 and n < 12:
                                attention(NPAIR - 1, n)
                            n += 1
            for kp in range(4):
                pe.wait_ge(S["mg_done"], 2 * kp + 2)
                rows_block(B_OUT + kp, kp, mg_hi, mg_lo, 4)

            def logits(t):
                if t == 0:
                    pe.wait_ge(S["route_in"], 80)
                pe.wait_ge(S["xn2T_done"], t + 1)
                for k in range(KD):
                    mm = pe.matmul(ps[:, 0, t * 32:t * 32 + NG + NE], xn2T[:, t % 2, k * P:(k + 1) * P],
                                   router_w[:, k, :], start=(k == 0), stop=(k == KD - 1))
                mm.then_inc(S["logits_ps"], 1)

            def turn_xn2(t):
                pe.wait_ge(S["xn2_done"], t + 1)
                if t >= 2:
                    pe.wait_ge(S["xn2T_done"], t - 1)
                for k in range(KD):
                    mm = pe.transpose(ps[:, 4 + 2 * (t % 2) + k // 4, (k % 4) * P:(k % 4 + 1) * P],
                                      xn2[:, t, k * P:(k + 1) * P], ident[:, :])
                mm.then_inc(S["xn2T_ps"], 1)

            for t in range(NT):
                for kp in range(4):
                    b = B_OUT + 4 + kp
                    if t == 0:
                        lo_wait(pe, b)
                    for kk in range(2):
                        k = 2 * kp + kk
                        mm = three(ps[:, t, :], mg_hi[:, k, t * P:(t + 1) * P], mg_lo[:, k, t * P:(t + 1) * P],
                                   w(b, 0)[:, kk * 512:(kk + 1) * 512], w(b, 1)[:, kk * 512:(kk + 1) * 512],
                                   k == 0, k == KD - 1)
                    if t == NT - 1:
                        mm.then_inc(S["w_used"], 1)
                    elif kp == 3:
                        mm.then_inc(S["x2_ps"], 1)
                if t >= 2:
                    logits(t - 2)
                if t >= 1:
                    turn_xn2(t - 1)
            turn_xn2(NT - 1)
            logits(NT - 2)
            logits(NT - 1)
            pe.wait_ge(S["picked"], 1)
            pe.wait_ge(S["consts_pool"], 3)
            for t in range(NT):
                for s in range(t + 1):
                    pe.matmul(ps[:, 1, t * NE:(t + 1) * NE], tri[:, 0 if s == t else 1, :], picked_bf[:, s, :],
                              start=(s == 0), stop=(s == t))
            for s in range(NT):
                mm = pe.matmul(ps[:, 1, NT * NE:(NT + 1) * NE], tri[:, 1, :], picked_bf[:, s, :],
                               start=(s == 0), stop=(s == NT - 1))
            mm.then_inc(S["counts_ps"], 1)

            def turn_x(rows, landed_in, count):
                pe.wait_ge(landed_in, count)
                for k in range(KD):
                    mm = pe.transpose(ps[:, 3 + k // 4, (k % 4) * P:(k % 4 + 1) * P],
                                      rows[:, k * P:(k + 1) * P], ident[:, :])
                mm.then_inc(S["xT_ps"], 1)

            def turn_h(n):
                pe.wait_ge(S["hid_done"], n)
                for k in range(DE // P):
                    mm = pe.transpose(ps[:, 2, k * P:(k + 1) * P], hid[:, k * P:(k + 1) * P], ident[:, :])
                mm.then_inc(S["hT_ps"], 1)

            def expert_block(slot, bank, k0, n_k, hi, lo):
                for kk in range(2):
                    k = k0 + kk
                    mm = three(ps[:, bank, :], hi[:, k, :], lo[:, k, :],
                               w_hi[:, slot, kk * 512:(kk + 1) * 512], w_lo[:, slot, kk * 512:(kk + 1) * 512],
                               k == 0, k == n_k - 1)
                mm.then_inc(S["w_used"], 1)

            pe.wait_ge(S["tile0_where"], 1)
            for k in range(KD):
                for t in range(NT):
                    mm = pe.matmul(ps[:, 3 + k // 4, (k % 4) * P:(k % 4 + 1) * P], xn2[:, t, k * P:(k + 1) * P],
                                   silu[:, t * P:(t + 1) * P], start=(t == 0), stop=(t == NT - 1))
            mm.then_inc(S["xT_ps"], 1)
            pe.wait_ge(S["xT_done"], 1)
            for r in range(8):
                lo_wait(pe, B_EXP + r)
                expert_block(r % HI_SLOTS, r // 4, 2 * (r % 4), KD, xT_hi, xT_lo)
            turn_x(x_odd, S["x_odd_in"], 16)
            def tile(at):
                i = at.i
                for r in range(PER_TILE):
                    if r == 0:
                        pe.wait_ge(S["xT_done"], i + 1)
                        pe.wait_ge(S["silu_done"], i)
                    if r == 4:
                        turn_h(i)
                    if r == 8:
                        turn_x(at.x, at.x_in, at.x_count)
                        pe.wait_ge(S["hT_done"], i)
                    lo_wait_loop(pe, i, r)
                    slot = (8 + r) % HI_SLOTS
                    if r < 8:
                        expert_block(slot, r // 4, 2 * (r % 4), KD, xT_hi, xT_lo)
                    else:
                        expert_block(slot, 5 + (r - 8) // 2, 2 * (r % 2), DE // P, hT_hi, hT_lo)

            tile(at_odd(0))
            with pe.Fori(1, PAIRED // 2) as q:
                tile(at_even(q))
                tile(at_odd(q))
            pe.wait_ge(S["tab"], 1)
            n_last = pe.value_load(tile_table[0:1, 0:1], min_val=NE - PAIRED + 1, max_val=MAX_TILES - PAIRED + 1)
            tiles = n_last + (PAIRED - 1)
            with pe.Fori(1, n_last) as n:
                tile(at_last(n))
            turn_h(tiles)
            pe.wait_ge(S["hT_done"], tiles)
            pe.wait_ge(S["y_act"], tiles)
            pe.wait_ge(S["y_dve"], tiles)
            for r in range(4):
                lo_wait_loop(pe, tiles, r)
                expert_block((8 + r) % HI_SLOTS, 5 + r // 2, 2 * (r % 2), DE // P, hT_hi, hT_lo)

        @block.vector
        def _(dve):
            chained = [0]

            def link(ins):
                chained[0] += 1
                ins.then_inc(S["dve_chain"], 1)
                dve.wait_ge(S["dve_chain"], chained[0])

            dve.sem_inc(S["lo_dve"], LO_DVE_0)
            dve.sem_inc(S["y_dve"], 1)
            dve.memset(wa_diag[:, :, :], 0.0).then_inc(S["consts_dve"], 1)
            dve.memset(wx_diag[:, :, :], 0.0).then_inc(S["consts_dve"], 1)
            dve.wait_ge(S["g1_in"], 16)
            def x_mean(t):
                dve.wait_ge(S["x0_sq_done"], t + 1)
                dve.tensor_scalar(stat[:, 0, t:t + 1], stat[:, 0, t:t + 1], 1.0 / D, EPS, ALU.mult, ALU.add)\
                   .then_inc(S["x0_stat"], 1)

            def x_lo(t):
                dve.wait_ge(S["xn_hi_done"], t + 1)
                dve.tensor_tensor(xn_lo[:, :, t * P:(t + 1) * P], turned_x(t),
                                  xn_hi[:, :, t * P:(t + 1) * P].bitcast(F32), ALU.subtract)\
                   .then_inc(S["xn_done"], 1)

            x_mean(0)
            for t in range(NT):
                if t + 1 < NT:
                    x_mean(t + 1)
                dve.wait_ge(S["x0_rstd"], t + 1)
                dve.scalar_tensor_tensor(out=x0[:, t, :], in0=x0[:, t, :], scalar=stat[:, 1, t:t + 1],
                                         in1=g1_rows[:, :], op0=ALU.mult, op1=ALU.mult)\
                   .then_inc(S["x0_norm"], 1)
                if t >= 2:
                    x_lo(t - 2)
            for t in range(NT - 2, NT):
                x_lo(t)
            dve.wait_ge(S["relb_in"], 16)
            dve.tensor_copy(probs[0:HEADS, 0, 0:P - 1],
                            probs[0:HEADS, 1, 2 * CLIP:2 * CLIP + 1].to_broadcast([HEADS, P - 1]))\
               .then_inc(S["toep_rev"], 1)
            dve.tensor_copy(probs[0:HEADS, 0, P - 1:3 * P], probs[0:HEADS, 1, 2 * CLIP::-1])\
               .then_inc(S["toep_rev"], 1)
            dve.wait_ge(S["sguT_ps"], 1)
            link(dve.tensor_copy(par[:, :], ps[:, 6, 0:N_PAR]))
            dve.tensor_copy(sgu_wT[:, :, :].rearrange("p g t -> p (g t)"), ps[:, 7, :])\
               .then_inc(S["sguT_done"], 1)

            lam = par[:, PAR_LAM:PAR_LAM + NPAIR]
            mag, e1, s1, s2, acc = (chan[:, n, :] for n in (0, 1, 4, 5, 6))
            link(dve.tensor_scalar(mag, lam, -1.0, None, ALU.mult))
            dve.tensor_tensor(mag, lam, mag, ALU.max).then_inc(S["sp_exp"], 1)
            dve.wait_ge(S["sp_exp"], 2)
            link(dve.tensor_scalar(s2, e1, 2.0, None, ALU.add))
            link(dve.reciprocal(s1, s2))
            link(dve.tensor_tensor(s1, s1, e1, ALU.mult))
            link(dve.tensor_tensor(s2, s1, s1, ALU.mult))
            terms = 9
            link(dve.tensor_scalar(acc, s2, 1.0 / (2 * terms + 1), 1.0 / (2 * terms - 1), ALU.mult, ALU.add))
            for n in range(terms - 2, -1, -1):
                link(dve.tensor_tensor(acc, acc, s2, ALU.mult))
                link(dve.tensor_scalar(acc, acc, 1.0 / (2 * n + 1), None, ALU.add))
            link(dve.tensor_tensor(acc, acc, s1, ALU.mult))
            link(dve.tensor_scalar(mag, lam, -1.0, 0.0, ALU.mult, ALU.max))
            link(dve.scalar_tensor_tensor(out=acc, in0=acc, scalar=2.0, in1=mag, op0=ALU.mult, op1=ALU.add))
            link(dve.tensor_scalar(chan[:, 3, :], acc, -LRU_C / 2, None, ALU.mult))
            dve.tensor_scalar(chan[:, 2, :], acc, LRU_C / 2, None, ALU.mult).then_inc(S["sp_done"], 1)
            link(dve.tensor_scalar(par[:, PAR_BA:PAR_BA + 2 * NPAIR], par[:, PAR_BA:PAR_BA + 2 * NPAIR], 0.5, None,
                                   ALU.mult))
            dve.tensor_scalar(par[:, PAR_GATE:N_PAR], par[:, PAR_GATE:N_PAR], 0.5, None, ALU.mult)\
               .then_inc(S["halved"], 1)
            dve.wait_ge(S["halved"], 1)
            link(dve.memset(xrT[:, 0:CONV - 1], 0.0))

            dve.wait_ge(S["sgu_in"], 32)
            for t in range(NT):
                dve.wait_ge(S["sv_sq"], t + 1)
                dve.tensor_scalar(stat[:, 2, t:t + 1], stat[:, 2, t:t + 1], 1.0 / AW, EPS, ALU.mult, ALU.add)\
                   .then_inc(S["sv_stat"], 1)
            for t in range(NT):
                dve.wait_ge(S["sv_rstd"], t + 1)
                dve.scalar_tensor_tensor(out=sv_rows[:, t, :], in0=sv_rows[:, t, :],
                                         scalar=stat[:, 3, t:t + 1], in1=sgu_g_sb[:, :],
                                         op0=ALU.mult, op1=ALU.mult).then_inc(S["sv_done"], 1)

            def bias_and_max(n):
                h, i = n // NT, n % NT
                w, buf, dst = P * (i + 1), n % 2, probs_of(n)
                dve.wait_ge(S["scores_ps"], n + 1)
                if n == 0:
                    dve.wait_ge(S["bias_done"], 1)
                if n >= 3:
                    dve.wait_ge(S["probsT_ps"], n - 2)
                near = min(2, i + 1) * P
                if w > near:
                    link(dve.tensor_scalar(dst[:, 0:w - near], ps[:, 4 + buf, 0:w - near], DH ** -0.5,
                                           bias[:, h, 0:1], ALU.mult, ALU.add))
                link(dve.scalar_tensor_tensor(out=dst[:, w - near:w], in0=ps[:, 4 + buf, w - near:w],
                                              scalar=DH ** -0.5, in1=bias[:, h, 2 * P - near:],
                                              op0=ALU.mult, op1=ALU.add))
                dve.tensor_reduce(att[:, n % 3, 0:1], dst[:, 0:w], AX.X, ALU.max, negate=True)\
                   .then_inc(S["biased"], 1)

            def normalise(n):
                w = P * (n % NT + 1)
                dve.wait_ge(S["exped"], n + 1)
                link(dve.reciprocal(att[:, n % 3, 2:3], att[:, n % 3, 1:2]))
                dve.tensor_scalar(probs_of(n)[:, 0:w], probs_of(n)[:, 0:w], att[:, n % 3, 2:3], None,
                                  ALU.mult).then_inc(S["normed"], 1)

            def attention(jp, u):
                if 2 <= u < 10:
                    normalise(8 * jp + u - 2)
                if u < 8:
                    bias_and_max(8 * jp + u)

            def a_out_lo(jp):
                dve.wait_ge(S["a_hi"], jp + 1)
                dve.tensor_tensor(br_lo[:, 0, jp, :], ps[:, 7, :], br_hi[:, 0, jp, :].bitcast(F32),
                                  ALU.subtract).then_inc(S["a_ready"], 1)

            def convolve(j, step):
                if step == 0:
                    dve.wait_ge(S["taken"], pair_block(j, XR) + 1)
                    if j > 0:
                        dve.wait_ge(S["c_mid"], j)
                    link(dve.tensor_scalar(conv[:, :], xrT[:, 0:TOK], par[:, PAR_CW + j:PAR_CW + j + 1], None,
                                           ALU.mult))
                elif step < CONV:
                    at = PAR_CW + NPAIR * step + j
                    link(dve.scalar_tensor_tensor(out=conv[:, :], in0=xrT[:, step:step + TOK],
                                                  scalar=par[:, at:at + 1], in1=conv[:, :],
                                                  op0=ALU.mult, op1=ALU.add))
                else:
                    dve.tensor_scalar(conv[:, :], conv[:, :], par[:, PAR_CB + j:PAR_CB + j + 1], None, ALU.add)\
                       .then_inc(S["conv_done"], 1)

            def recurrence_in(j):
                dve.wait_ge(S["gates_done"], 2 * j + 2)
                link(dve.scalar_tensor_tensor(out=igate[:, :], in0=igate[:, :], scalar=1.0, in1=conv[:, :],
                                              op0=ALU.add, op1=ALU.mult))
                dve.wait_ge(S["decay_done"], 2 * j + 2)
                link(dve.tensor_tensor(conv[:, :], decay[:, :], decay[:, :], ALU.mult))
                link(dve.scalar_tensor_tensor(out=rgate[:, :], in0=conv[:, :], scalar=1.0, in1=rgate[:, :],
                                              op0=ALU.add, op1=ALU.mult))
                dve.tensor_scalar(rgate[:, :], rgate[:, :], 0.0, None, ALU.max).then_inc(S["mult_in"], 1)

            def recurrence(j):
                dve.wait_ge(S["mult_done"], j + 1)
                link(dve.scalar_tensor_tensor(out=igate[:, :], in0=igate[:, :], scalar=0.5, in1=rgate[:, :],
                                              op0=ALU.mult, op1=ALU.mult))
                link(dve.tensor_tensor_scan(out=conv[:, :], data0=decay[:, :], data1=igate[:, :], initial=0.0,
                                            op0=ALU.mult, op1=ALU.add))

            def c_out(j):
                dve.wait_ge(S["taken"], pair_block(j, XG) + 1)
                dve.tensor_tensor(gx[:, :], gx[:, :], conv[:, :], ALU.mult).then_inc(S["c_mid"], 1)

            def b_out(j):
                dve.wait_ge(S["mix_ps"], j + 1)
                dve.wait_ge(S["u_done"], j + 1)
                link(dve.tensor_tensor(rgate[:, :].rearrange("p (n t) -> p n t", n=NT),
                                       ps[:, 2, :].rearrange("p (n t) -> p n t", n=NT),
                                       sgu_b_sb[:, j, :].unsqueeze(1).to_broadcast([P, NT, P]), ALU.add))
                dve.tensor_tensor(gu[:, :], gu[:, :], rgate[:, :], ALU.mult).then_inc(S["b_mid"], 1)

            def lo_parts(j):
                dve.wait_ge(S["ch"], j + 1)
                dve.tensor_tensor(br_lo[:, 2, j, :], gx[:, :], br_hi[:, 2, j, :].bitcast(F32), ALU.subtract)\
                   .then_inc(S["c_ready"], 1)
                dve.wait_ge(S["bh"], j + 1)
                dve.tensor_tensor(br_lo[:, 1, j, :], gu[:, :], br_hi[:, 1, j, :].bitcast(F32), ALU.subtract)\
                   .then_inc(S["b_ready"], 1)

            for j in range(NPAIR):
                for r in range(PER_PAIR):
                    if r == XR and j > 0:
                        c_out(j - 1)
                    for n in range(3 * r, 3 * r + 3):
                        if 4 <= n <= 7:
                            convolve(j, n - 4)
                            if n == 7:
                                convolve(j, CONV)
                        if j > 0:
                            attention(j - 1, n)
                    if r == UU:
                        if j > 0:
                            lo_parts(j - 1)
                            a_out_lo(j - 1)
                        recurrence_in(j)
                    if r == XG:
                        recurrence(j)
                        b_out(j)

            def gated(m, o, c):
                g = 6 * m + 2 * o + c
                k = 2 * m + c
                dve.wait_ge(S["w_used"], out_block(m, 3 * o + 2) + 1)
                dve.wait_ge(S["gate_ready"], g + 1)
                if o == 0:
                    if m > 0:
                        dve.wait_ge(S["mg_done"], k - 1)
                    dve.scalar_tensor_tensor(out=macc_of(k), in0=gate_buf[:, g % 3, :], scalar=1.0,
                                             in1=ps[:, 2 + c, :], op0=ALU.add, op1=ALU.mult)\
                       .then_inc(S["wb_taken"], 1)
                    return
                dve.scalar_tensor_tensor(out=macc[:, 1, :], in0=gate_buf[:, g % 3, :], scalar=1.0,
                                         in1=ps[:, 2 + c, :], op0=ALU.add, op1=ALU.mult)\
                   .then_inc(S["wb_taken"], 1)
                dve.wait_ge(S["wb_taken"], g + 1)
                add = dve.tensor_tensor(macc_of(k), macc_of(k), macc[:, 1, :], ALU.add)
                if o == 2:
                    add.then_inc(S["macc_done"], 1)
                    dve.wait_ge(S["macc_done"], k + 1)
                else:
                    link(add)

            def mg_lo_part(k):
                dve.wait_ge(S["mg_hi_done"], k + 1)
                dve.scalar_tensor_tensor(out=mg_lo[:, k, :], in0=macc_of(k), scalar=0.5,
                                         in1=mg_hi[:, k, :].bitcast(F32), op0=ALU.mult, op1=ALU.subtract)\
                   .then_inc(S["mg_done"], 1)

            for m in range(NPAIR):
                n = 0
                for r in range(PER_OUT):
                    if m == 0 and r == 0:
                        c_out(NPAIR - 1)
                    if r % 3 == 0 and r > 0:
                        for c in range(2):
                            gated(m, r // 3 - 1, c)
                    if m == 0:
                        for _ in range(2 if r % 3 == 2 else 3):
                            if n < 10:
                                attention(NPAIR - 1, n)
                            n += 1
                        if r == 1:
                            lo_parts(NPAIR - 1)
                        if r == 5:
                            a_out_lo(NPAIR - 1)
                for c in range(2):
                    gated(m, 2, c)
                for c in range(2):
                    mg_lo_part(2 * m + c)
            dve.wait_ge(S["x_again"], 16)
            dve.wait_ge(S["w_used"], B_OUT + 4)
            for t in range(NT):
                dve.tensor_tensor(x_rows[:, t, 0:512], ps[:, 4 + t, :], x_rows[:, t, 0:512], ALU.add)\
                   .then_inc(S["x2_done"], 1)
            dve.wait_ge(S["g2_in"], 16)
            for t in range(NT):
                if t < NT - 1:
                    dve.wait_ge(S["x2_ps"], t + 1)
                else:
                    dve.wait_ge(S["w_used"], B_EXP)
                dve.tensor_tensor(x_rows[:, t, 512:1024], ps[:, t, :], x_rows[:, t, 512:1024], ALU.add)\
                   .then_inc(S["x2_done"], 1)
                dve.wait_ge(S["x2_sq"], t + 1)
                dve.tensor_scalar(stat[:, 4, t:t + 1], stat[:, 4, t:t + 1], 1.0 / D, EPS, ALU.mult, ALU.add)\
                   .then_inc(S["x2_stat"], 1)
                dve.wait_ge(S["x2_rstd"], t + 1)
                dve.scalar_tensor_tensor(out=xn2[:, t, :], in0=x_rows[:, t, :], scalar=stat[:, 5, t:t + 1],
                                         in1=g2_rows[:, :], op0=ALU.mult, op1=ALU.mult)\
                   .then_inc(S["xn2_done"], 1)

            def row(n, *shape):
                size = 1
                for x in shape:
                    size *= x
                flat = route[:, n:n + 2, :].rearrange("p a b -> p (a b)")[:, 0:size] if size > NT * NE \
                    else route[:, n, 0:size]
                if len(shape) == 2:
                    return flat.rearrange("p (a b) -> p a b", a=shape[0])
                if len(shape) == 3:
                    return flat.rearrange("p (a b c) -> p a b c", a=shape[0], b=shape[1])
                return flat

            def spread(x, *shape):
                return x.unsqueeze(2).to_broadcast([P, *shape])

            def first_of(dst, x, best, weight, scratch, top, n):
                link(dve.tensor_tensor(scratch, x, spread(best, NT, n), ALU.is_equal))
                link(dve.tensor_tensor(scratch, scratch, weight, ALU.mult))
                link(dve.tensor_reduce(top, scratch, AX.X, ALU.max))
                link(dve.tensor_tensor(dst, scratch, spread(top, NT, n), ALU.is_equal))

            def four(n):
                return route[:, 2, NT * n:NT * (n + 1)]

            falling4, falling16 = row(20, NT, NG), row(21, NT, NE)
            tile_start, count8, count16 = row(22, NE), row(23, 8), row(24, NE)
            zeros16 = row(25, NE)
            link(dve.memset(zeros16, 0.0))
            both = row(0, NT, NG + NE)
            dve.wait_ge(S["consts_pool"], 9)
            dve.wait_ge(S["logits_ps"], NT)
            link(dve.tensor_tensor(both, ps[:, 0, 0:NT * 32].rearrange("p (t n) -> p t n", n=32)[:, :, 0:NG + NE],
                                   router_b[:, :].unsqueeze(1).to_broadcast([P, NT, NG + NE]), ALU.add))
            g_log = both[:, :, 0:NG]
            g_max, g_top, g_sum, e_max, e_top, e_max2, e_sum, scale_t, s_first, s_second = (
                four(n) for n in range(10))
            link(dve.tensor_reduce(g_max, g_log, AX.X, ALU.max))
            dve.tensor_tensor(row(3, NT, NG), g_log, spread(g_max, NT, NG), ALU.subtract)\
               .then_inc(S["gexp_in"], 1)
            g_sel = row(6, NT, NG)
            first_of(g_sel, g_log, g_max, falling4, row(5, NT, NG), g_top, NG)
            link(dve.tensor_scalar(g_sel, g_sel, -1.0, -NEG, ALU.add, ALU.mult))
            e_log = row(7, NT, NE)
            link(dve.tensor_tensor(row(7, NT, NG, EPG),
                                   both[:, :, NG:].rearrange("p t (g e) -> p t g e", g=NG),
                                   g_sel.unsqueeze(3).to_broadcast([P, NT, NG, EPG]), ALU.add))
            link(dve.tensor_reduce(e_max, e_log, AX.X, ALU.max))
            dve.tensor_tensor(row(11, NT, NE), e_log, spread(e_max, NT, NE), ALU.subtract)\
               .then_inc(S["gexp_in"], 1)
            sel1, sel2 = row(8, NT, NE), row(9, NT, NE)
            first_of(sel1, e_log, e_max, falling16, row(10, NT, NE), e_top, NE)
            link(dve.scalar_tensor_tensor(out=e_log, in0=sel1, scalar=NEG, in1=e_log, op0=ALU.mult, op1=ALU.add))
            link(dve.tensor_reduce(e_max2, e_log, AX.X, ALU.max))
            first_of(sel2, e_log, e_max2, falling16, row(10, NT, NE), e_top, NE)
            link(dve.tensor_tensor(sel1, sel1, sel2, ALU.add))
            dve.tensor_copy(picked_bf[:, :, :], sel1).then_inc(S["picked"], 1)
            before = ps[:, 1, 0:NT * NE].rearrange("p (t n) -> p t n", n=NE)
            far = float(2 * SLOT_TILES * P)
            slot0 = four(10)
            link(dve.tensor_scalar(slot0.unsqueeze(2), sel1[:, :, 0:1], -float(far), float(far), ALU.mult, ALU.add))
            dve.wait_ge(S["counts_ps"], 1)
            link(dve.tensor_tensor(slot0.unsqueeze(2), slot0.unsqueeze(2), before[:, :, 0:1], ALU.add))
            dve.tensor_tensor(silu[:, :].rearrange("p (t s) -> p t s", t=NT),
                              hid[:, 0:P].unsqueeze(1).to_broadcast([P, NT, P]), spread(slot0, NT, P),
                              ALU.is_equal).then_inc(S["tile0_where"], 1)
            more, upto, base = row(13, NE), row(14, NE), row(15, NE)
            total = ps[:, 1, NT * NE:(NT + 1) * NE]
            link(dve.tensor_scalar(more, total, float(P), None, ALU.is_gt))
            for n in range(2, NT):
                link(dve.scalar_tensor_tensor(out=more, in0=total, scalar=float(n * P), in1=more,
                                              op0=ALU.is_gt, op1=ALU.add))
            link(dve.tensor_tensor_scan(out=upto, data0=more, data1=zeros16, initial=0.0,
                                        op0=ALU.add, op1=ALU.add))
            link(dve.tensor_tensor(base, upto, more, ALU.subtract))
            link(dve.tensor_scalar(base, base, float(P), float((NE - 1) * P), ALU.mult, ALU.add))
            link(dve.tensor_tensor(base, base, tile_start, ALU.subtract))
            slot, late = row(16, NT, NE), row(17, NT, NE)
            link(dve.tensor_scalar(late, before, float(P), None, ALU.is_ge))
            link(dve.tensor_tensor(late, late, base.unsqueeze(1).to_broadcast([P, NT, NE]), ALU.mult))
            link(dve.tensor_tensor(slot, before, tile_start.unsqueeze(1).to_broadcast([P, NT, NE]), ALU.add))
            link(dve.tensor_tensor(slot, slot, late, ALU.add))
            link(dve.scalar_tensor_tensor(out=late, in0=slot, scalar=-far, in1=sel1, op0=ALU.add, op1=ALU.mult))
            link(dve.tensor_reduce(s_first, late, AX.X, ALU.min))
            link(dve.tensor_scalar(s_first, s_first, far, None, ALU.add))
            link(dve.tensor_tensor(late, slot, sel1, ALU.mult))
            link(dve.tensor_reduce(s_second, late, AX.X, ALU.max))
            idx = slot_idx[:, :].rearrange("p (t k) -> p t k", k=2)
            dve.tensor_copy(idx[:, :, 0:1], s_first.unsqueeze(2))
            dve.tensor_copy(idx[:, :, 1:2], s_second.unsqueeze(2)).then_inc(S["routed"], 1)
            link(dve.tensor_scalar(late[:, 0, 0:1], upto[:, NE - 1:NE], float(NE - PAIRED + 1), None, ALU.add))
            dve.tensor_copy(tile_table[:, 0:1], late[:, 0, 0:1])
            dve.tensor_copy(tile_table[:, 1:NE + 1], count16)
            over = row(18, 8, NE)
            link(dve.tensor_tensor(over, upto.unsqueeze(1).to_broadcast([P, 8, NE]),
                                   count8.unsqueeze(2).to_broadcast([P, 8, NE]), ALU.is_le))
            dve.wait_ge(S["gexp_done"], 1)
            link(dve.tensor_reduce(row(3, 8), over, AX.X, ALU.add))
            link(dve.tensor_scalar(row(3, 8), row(3, 8), float(NE - 1), None, ALU.min))
            dve.tensor_copy(tile_table[:, NE + 1:NE + 9], row(3, 8)).then_inc(S["tab"], 1)
            comb = row(12, NT, NE)
            dve.wait_ge(S["eexp_done"], 1)
            link(dve.tensor_tensor(comb, comb, sel1, ALU.mult))
            link(dve.tensor_reduce(e_sum, comb, AX.X, ALU.add))
            link(dve.tensor_reduce(g_sum, row(4, NT, NG), AX.X, ALU.add))
            link(dve.tensor_tensor(scale_t, g_sum, e_sum, ALU.mult))
            link(dve.reciprocal(scale_t, scale_t))
            link(dve.tensor_tensor(comb, comb, spread(scale_t, NT, NE), ALU.mult))
            for k, s in enumerate((s_first, s_second)):
                link(dve.tensor_tensor(late, slot, spread(s, NT, NE), ALU.is_equal))
                link(dve.tensor_tensor(late, late, comb, ALU.mult))
                link(dve.tensor_reduce(w_first[:, k, :], late, AX.X, ALU.add))

            def xT_lo_part(n):
                dve.wait_ge(S["xT_hi_done"], n)
                dve.tensor_tensor(xT_lo[:, :, :].rearrange("p k n -> p (k n)"),
                                  ps[:, 3:5, :].rearrange("p a n -> p (a n)"),
                                  xT_hi[:, :, :].rearrange("p k n -> p (k n)").bitcast(F32), ALU.subtract)\
                   .then_inc(S["xT_done"], 1)

            def hT_lo_part(n):
                dve.wait_ge(S["hT_hi_done"], n)
                dve.tensor_tensor(hT_lo[:, :, :].rearrange("p k n -> p (k n)"), ps[:, 2, :],
                                  hT_hi[:, :, :].rearrange("p k n -> p (k n)").bitcast(F32), ALU.subtract)\
                   .then_inc(S["hT_done"], 1)

            def hidden(used, n):
                dve.wait_ge(S["w_used"], used)
                dve.wait_ge(S["silu_done"], n)
                dve.tensor_tensor(hid[:, :], silu[:, :], ps[:, 1, :], ALU.mult).then_inc(S["hid_done"], 1)

            xT_lo_part(1)
            for r in range(AHEAD, 8):
                if not on_pool(r):
                    split_lo(dve, B_EXP + r)
            for r in range(8, 8 + AHEAD):
                if not on_pool(r):
                    split_lo_loop(dve, at_odd(0), r - 8)
            hidden(B_EXP + 8, 1)
            xT_lo_part(2)
            def tile(at):
                i = at.i
                for r in range(PER_TILE):
                    if not on_pool(8 + r + AHEAD):
                        split_lo_loop(dve, at, r + AHEAD)
                    if r == 5:
                        hT_lo_part(i)
                    if r == 8:
                        dve.wait_ge(S["hT_ps"], i)
                        hidden(loop_block(i, 8), i + 1)
                    if r == 9:
                        xT_lo_part(i + 2)
                dve.wait_ge(S["w_used"], loop_block(i, PER_TILE))
                dve.wait_ge(at.y_free, at.y_count)
                dve.tensor_copy(at.y[:, 512:1024], ps[:, 6, :]).then_inc(S["y_dve"], 1)

            tile(at_odd(0))
            with dve.Fori(1, PAIRED // 2) as q:
                tile(at_even(q))
                tile(at_odd(q))
            dve.wait_ge(S["tab"], 1)
            n_last = dve.value_load(tile_table[0:1, 0:1], min_val=NE - PAIRED + 1, max_val=MAX_TILES - PAIRED + 1)
            tiles = n_last + (PAIRED - 1)
            with dve.Fori(1, n_last) as n:
                tile(at_last(n))
            hT_lo_part(tiles)
            if not on_pool(8 + AHEAD):
                split_lo_loop(dve, at_last(n_last), AHEAD)
            dve.wait_ge(S["w_used"], loop_block(tiles, 4))
            dve.wait_ge(S["y_last_stored"], n_last * 16)
            dve.tensor_copy(y_tile[:, 512:1024], ps[:, 6, :]).then_inc(S["y_dve"], 1)
            for t in range(NT):
                dve.wait_ge(got_in[0][t], 16)
                dve.scalar_tensor_tensor(out=y_lo(t), in0=y_lo(t), scalar=w_first[:, 0, t:t + 1],
                                         in1=x_rows[:, t, :], op0=ALU.mult, op1=ALU.add)\
                   .then_inc(S["y_sum"], 1)

            def last_mean(t):
                dve.wait_ge(S["y_sq"], t + 1)
                dve.tensor_scalar(stat[:, 6, t:t + 1], stat[:, 6, t:t + 1], 1.0 / D, EPS, ALU.mult, ALU.add)\
                   .then_inc(S["y_stat"], 1)

            def last_norm(t):
                dve.wait_ge(S["y_rstd"], t + 1)
                dve.scalar_tensor_tensor(out=y_lo(t), in0=y_lo(t), scalar=stat[:, 7, t:t + 1],
                                         in1=gf_rows[:, :], op0=ALU.mult, op1=ALU.mult)\
                   .then_inc(S["y_norm"], 1)

            for t in range(NT):
                dve.wait_ge(got_in[1][t], 16)
                dve.wait_ge(S["y_sum"], t + 1)
                dve.scalar_tensor_tensor(out=y_lo(t), in0=y_hi(t), scalar=w_first[:, 1, t:t + 1],
                                         in1=y_lo(t), op0=ALU.mult, op1=ALU.add).then_inc(S["y_sum"], 1)
                if t >= 1:
                    last_mean(t - 1)
                if t >= 2:
                    last_norm(t - 2)
            last_mean(NT - 1)
            last_norm(NT - 2)
            last_norm(NT - 1)


_INS = ("x", "norm1_g", "w_in", "b_gate", "rel_bias", "sgu_norm_g", "sgu_w", "sgu_b", "conv_w", "conv_b",
        "rg_wa", "rg_ba", "rg_wx", "rg_bx", "rg_lambda", "w_branch", "w_out", "norm2_g", "router_grp_w",
        "router_grp_b", "router_exp_w", "router_exp_b", "exp_w_gate", "exp_w_up", "exp_w_down", "final_norm_g")


def kernel(**inputs):
    import numpy as np
    import concourse.bacc as bacc
    from concourse.bass_utils import run_bass_kernel_spmd

    nc = bacc.Bacc("TRN2", target_bir_lowering=False, num_devices=1)
    arrays, args = {}, {}
    for name in _INS:
        x = np.ascontiguousarray(inputs[name])
        arrays[f"in_{name}"] = x
        args[name] = nc.dram_tensor(f"in_{name}", x.shape, mybir.dt.from_np(x.dtype), kind="ExternalInput").ap()
    out = nc.dram_tensor("out", (1, TOK, D), F32, kind="ExternalOutput").ap()
    build(nc, args, out)
    r = run_bass_kernel_spmd(nc, [arrays], core_ids=[0])
    return r.results[0]["out"]
```
